# Optimizing a Trainium2 kernel written in Bass

```python
import functools
import jax, jax.numpy as jnp
from jax import lax
import numpy as np

D_MODEL = 1024
BATCH = 1
SEQ = 1024
DEPTH = 2
DEC_BATCH = 8
DEC_SEQ = 8
PAST_LEN = 1024
PAGE_SIZE = 128

N_EVEN = (DEPTH + 1) // 2
N_ODD = DEPTH // 2
H_A = 8
HD_A = 64
W_A = H_A * HD_A
H_B = 8
BW_B = 64
W_B = H_B * BW_B
CONV_B = 4
C_LRU = 8.0
H_C = 8
CW_C = 128
W_C = H_C * CW_C
CHUNK = 128
D_FF = 3 * D_MODEL
CONV_F = 3
Q_BLOCK = 128
EPS = 1e-6
D_IN_EVEN = 3 * W_A + 2 * W_B

kernel_name = "stickbreak_rglru_chunkmlp_convffn_step"

def rmsnorm(x, g):
    xf = x.astype(jnp.float32)
    y = xf * lax.rsqrt(jnp.mean(xf * xf, axis=-1, keepdims=True) + EPS)
    return (y * g.astype(jnp.float32)).astype(x.dtype)

def causal_dwconv(x, buf, w, b):
    width = w.shape[0]
    t = x.shape[1]
    xp = jnp.concatenate([buf.astype(x.dtype), x], axis=1)
    y = b
    for j in range(width):
        y = y + w[j] * xp[:, j:j + t]
    return y, xp[:, xp.shape[1] - (width - 1):]

def sb_attend(q, k, v, bias, q_pos, k_pos):
    z = (jnp.einsum('bqhd,bkhd->bhqk', q, k).astype(jnp.float32) * (HD_A ** -0.5)
         + bias.astype(jnp.float32)[None, :, None, None])
    causal = k_pos[None, :] < q_pos[:, None]
    log_keep = jnp.where(causal, jax.nn.log_sigmoid(-z), 0.0)
    log_after = lax.cumsum(log_keep, axis=3, reverse=True) - log_keep
    w = jnp.where(causal, jnp.exp(jax.nn.log_sigmoid(z) + log_after), 0.0)
    return jnp.einsum('bhqk,bkhd->bqhd', w.astype(v.dtype), v)

def sb_prompt(q, k, v, bias):
    b, t, h, d = q.shape
    nb = t // Q_BLOCK
    qb = jnp.moveaxis(q.reshape(b, nb, Q_BLOCK, h, d), 1, 0)
    qpos = jnp.arange(t, dtype=jnp.int32).reshape(nb, Q_BLOCK)
    kpos = jnp.arange(t, dtype=jnp.int32)
    ob = lax.map(lambda a: sb_attend(a[0], k, v, bias, a[1], kpos), (qb, qpos))
    return jnp.moveaxis(ob, 0, 1).reshape(b, t, h, d)

def sb_cached(q, k, v, bias, k_past, v_past):
    past = k_past.shape[1]
    t = q.shape[1]
    k_all = jnp.concatenate([k_past.astype(k.dtype), k], axis=1)
    v_all = jnp.concatenate([v_past.astype(v.dtype), v], axis=1)
    q_pos = past + jnp.arange(t, dtype=jnp.int32)
    k_pos = jnp.arange(past + t, dtype=jnp.int32)
    return sb_attend(q, k_all, v_all, bias, q_pos, k_pos)

def _lin_combine(prev, nxt):
    a1, b1 = prev
    a2, b2 = nxt
    return a1 * a2, a2 * b1 + b2

def rglru(xc, h0, w_r, b_r, w_i, b_i, lam):
    b, t, _ = xc.shape
    xf = xc.astype(jnp.float32).reshape(b, t, H_B, BW_B)
    r = jax.nn.sigmoid(jnp.einsum('bthc,hcd->bthd', xf, w_r.astype(jnp.float32)) + b_r)
    i = jax.nn.sigmoid(jnp.einsum('bthc,hcd->bthd', xf, w_i.astype(jnp.float32)) + b_i)
    log_a = -C_LRU * r * jax.nn.softplus(-lam.astype(jnp.float32))
    a = jnp.exp(log_a).reshape(b, t, W_B)
    u = (jnp.sqrt(-jnp.expm1(2.0 * log_a)) * (i * xf)).reshape(b, t, W_B)
    u = u.at[:, 0].add(a[:, 0] * h0.astype(jnp.float32))
    _, h = lax.associative_scan(_lin_combine, (a, u), axis=1)
    return h.astype(xc.dtype), h[:, -1].astype(xc.dtype)

def even_mixer(xn, h0, conv_buf, attend, w_in, gq, gk, sb_bias, w_conv, b_conv, w_r, b_r, w_i, b_i, lam, w_out):
    b, t, _ = xn.shape
    proj = xn @ w_in
    q, k, v, xb, gb = jnp.split(proj, [W_A, 2 * W_A, 3 * W_A, 3 * W_A + W_B], axis=-1)
    q = rmsnorm(q.reshape(b, t, H_A, HD_A), gq)
    k = rmsnorm(k.reshape(b, t, H_A, HD_A), gk)
    v = v.reshape(b, t, H_A, HD_A)
    o_a = attend(q, k, v, sb_bias).reshape(b, t, W_A)
    xc, new_buf = causal_dwconv(xb, conv_buf, w_conv, b_conv)
    h, h_last = rglru(xc, h0, w_r, b_r, w_i, b_i, lam)
    o_b = h * jax.nn.gelu(gb)
    out = jnp.concatenate([o_a, o_b], axis=-1) @ w_out
    return out, k, v, h_last, new_buf

def chunk_mix(v, w_s, b_s):
    b, t, h, c = v.shape
    nc = -(-t // CHUNK)
    vp = jnp.pad(v, ((0, 0), (0, nc * CHUNK - t), (0, 0), (0, 0))).reshape(b, nc, CHUNK, h, c)
    w = w_s * jnp.tril(jnp.ones((CHUNK, CHUNK), w_s.dtype))
    o = jnp.einsum('hts,bnshc->bnthc', w, vp) + jnp.swapaxes(b_s, 0, 1)[:, :, None]
    return o.reshape(b, nc * CHUNK, h, c)[:, :t]

def odd_mixer(xn, w_in, gv, w_s, b_s, w_out):
    b, t, _ = xn.shape
    z = jax.nn.gelu(xn @ w_in)
    u, v = jnp.split(z, 2, axis=-1)
    v = rmsnorm(v.reshape(b, t, H_C, CW_C), gv.reshape(H_C, CW_C))
    vm = chunk_mix(v, w_s, b_s).reshape(b, t, W_C)
    return (u * vm) @ w_out, v.reshape(b, t, W_C)

def conv_ffn(xn, buf, w_g, w_u, w_c, b_c, w_d):
    g = xn @ w_g
    gc, new_buf = causal_dwconv(g, buf, w_c, b_c)
    return (jax.nn.gelu(gc) * (xn @ w_u)) @ w_d, new_buf

def setup_inputs(seed: int = 0) -> dict:
    key = jax.random.key(seed)
    ks = iter(jax.random.split(key, 48))
    f32 = jnp.float32

    def nrm(shape, scale):
        return jax.random.normal(next(ks), shape, f32) * scale

    n_pages = PAST_LEN // PAGE_SIZE
    n_used = DEC_BATCH * n_pages
    n_pool = (n_used * 5) // 4
    perm = jax.random.permutation(next(ks), n_pool)
    page_table = perm[:n_used].reshape(DEC_BATCH, n_pages).astype(jnp.int32)

    u = jax.random.uniform(next(ks), (N_EVEN, H_B, BW_B), f32, minval=0.9, maxval=0.999)
    sig = u ** (1.0 / C_LRU)
    lru_lambda = jnp.log(sig) - jnp.log1p(-sig)
    sb_bias = jax.random.uniform(next(ks), (N_EVEN, H_A), f32, minval=-8.0, maxval=-6.0)

    return {
        "x_prompt": nrm((BATCH, SEQ, D_MODEL), 1.0),
        "x_sample": nrm((DEC_BATCH, DEC_SEQ, D_MODEL), 1.0),
        "cache_k": nrm((N_EVEN, n_pool, PAGE_SIZE, H_A, HD_A), 1.0),
        "cache_v": nrm((N_EVEN, n_pool, PAGE_SIZE, H_A, HD_A), 1.0),
        "state_lru_h": nrm((N_EVEN, DEC_BATCH, W_B), 0.5),
        "state_lru_conv": nrm((N_EVEN, DEC_BATCH, CONV_B - 1, W_B), 1.0),
        "state_ffn_conv": nrm((DEPTH, DEC_BATCH, CONV_F - 1, D_FF), 1.0),
        "page_table": page_table,
        "g_mix": 1.0 + nrm((DEPTH, D_MODEL), 0.02),
        "g_ffn": 1.0 + nrm((DEPTH, D_MODEL), 0.02),
        "w_in_even": nrm((N_EVEN, D_MODEL, D_IN_EVEN), D_MODEL ** -0.5),
        "g_q": 1.0 + nrm((N_EVEN, HD_A), 0.02),
        "g_k": 1.0 + nrm((N_EVEN, HD_A), 0.02),
        "sb_bias": sb_bias,
        "w_conv_lru": nrm((N_EVEN, CONV_B, W_B), CONV_B ** -0.5),
        "b_conv_lru": nrm((N_EVEN, W_B), 0.02),
        "w_rgate": nrm((N_EVEN, H_B, BW_B, BW_B), BW_B ** -0.5),
        "b_rgate": nrm((N_EVEN, H_B, BW_B), 0.02),
        "w_igate": nrm((N_EVEN, H_B, BW_B, BW_B), BW_B ** -0.5),
        "b_igate": nrm((N_EVEN, H_B, BW_B), 0.02),
        "lru_lambda": lru_lambda,
        "w_out_even": nrm((N_EVEN, W_A + W_B, D_MODEL), (W_A + W_B) ** -0.5),
        "w_in_odd": nrm((N_ODD, D_MODEL, 2 * W_C), D_MODEL ** -0.5),
        "g_v": 1.0 + nrm((N_ODD, W_C), 0.02),
        "w_spatial": nrm((N_ODD, H_C, CHUNK, CHUNK), CHUNK ** -0.5),
        "b_spatial": 1.0 + nrm((N_ODD, H_C, CHUNK), 0.1),
        "w_out_odd": nrm((N_ODD, W_C, D_MODEL), W_C ** -0.5),
        "w_gate": nrm((DEPTH, D_MODEL, D_FF), D_MODEL ** -0.5),
        "w_up": nrm((DEPTH, D_MODEL, D_FF), D_MODEL ** -0.5),
        "w_ffn_conv": nrm((DEPTH, CONV_F, D_FF), CONV_F ** -0.5),
        "b_ffn_conv": nrm((DEPTH, D_FF), 0.02),
        "w_down": nrm((DEPTH, D_FF, D_MODEL), D_FF ** -0.5),
    }

def reference(x_prompt, x_sample, cache_k, cache_v, state_lru_h, state_lru_conv, state_ffn_conv, page_table,
              g_mix, g_ffn, w_in_even, g_q, g_k, sb_bias, w_conv_lru, b_conv_lru, w_rgate, b_rgate, w_igate, b_igate,
              lru_lambda, w_out_even, w_in_odd, g_v, w_spatial, b_spatial, w_out_odd,
              w_gate, w_up, w_ffn_conv, b_ffn_conv, w_down):
    bp, tp = x_prompt.shape[0], x_prompt.shape[1]
    bs = x_sample.shape[0]
    n_pages = page_table.shape[1]
    past = n_pages * PAGE_SIZE
    yp, ys = x_prompt, x_sample
    h0_p = jnp.zeros((bp, W_B), x_prompt.dtype)
    cbuf_p = jnp.zeros((bp, CONV_B - 1, W_B), x_prompt.dtype)
    fbuf_p = jnp.zeros((bp, CONV_F - 1, D_FF), x_prompt.dtype)
    last_chunk_start = ((tp - 1) // CHUNK) * CHUNK
    kp_l, vp_l, ks_l, vs_l, hp_l, hs_l, cp_l, cs_l = [], [], [], [], [], [], [], []
    chp_l, chs_l, fp_l, fs_l = [], [], [], []
    for l in range(DEPTH):
        if l % 2 == 0:
            e = l // 2
            ev = (w_in_even[e], g_q[e], g_k[e], sb_bias[e], w_conv_lru[e], b_conv_lru[e], w_rgate[e], b_rgate[e],
                  w_igate[e], b_igate[e], lru_lambda[e], w_out_even[e])
            k_past = cache_k[e][page_table].reshape(bs, past, H_A, HD_A)
            v_past = cache_v[e][page_table].reshape(bs, past, H_A, HD_A)
            attend_s = functools.partial(sb_cached, k_past=k_past, v_past=v_past)
            m_p, k_p, v_p, h_p, c_p = even_mixer(rmsnorm(yp, g_mix[l]), h0_p, cbuf_p, sb_prompt, *ev)
            m_s, k_s, v_s, h_s, c_s = even_mixer(rmsnorm(ys, g_mix[l]), state_lru_h[e], state_lru_conv[e],
                                                 attend_s, *ev)
            kp_l.append(k_p); vp_l.append(v_p); ks_l.append(k_s); vs_l.append(v_s)
            hp_l.append(h_p); hs_l.append(h_s); cp_l.append(c_p); cs_l.append(c_s)
        else:
            o = l // 2
            od = (w_in_odd[o], g_v[o], w_spatial[o], b_spatial[o], w_out_odd[o])
            m_p, vr_p = odd_mixer(rmsnorm(yp, g_mix[l]), *od)
            m_s, vr_s = odd_mixer(rmsnorm(ys, g_mix[l]), *od)
            chp_l.append(vr_p[:, last_chunk_start:]); chs_l.append(vr_s)
        yp = yp + m_p
        ys = ys + m_s
        fw = (w_gate[l], w_up[l], w_ffn_conv[l], b_ffn_conv[l], w_down[l])
        f_p, fb_p = conv_ffn(rmsnorm(yp, g_ffn[l]), fbuf_p, *fw)
        f_s, fb_s = conv_ffn(rmsnorm(ys, g_ffn[l]), state_ffn_conv[l], *fw)
        yp = yp + f_p
        ys = ys + f_s
        fp_l.append(fb_p); fs_l.append(fb_s)
    return (yp, ys,
            jnp.stack(kp_l), jnp.stack(vp_l), jnp.stack(ks_l), jnp.stack(vs_l),
            jnp.stack(hp_l), jnp.stack(hs_l), jnp.stack(cp_l), jnp.stack(cs_l),
            jnp.stack(chp_l), jnp.stack(chs_l), jnp.stack(fp_l), jnp.stack(fs_l))


_drawn_inputs = setup_inputs


def setup_inputs(seed=0):
    import zlib

    import numpy as np

    out = dict(_drawn_inputs(seed))
    spreads = {}
    factors = {'g_q': 8.0,
     'g_k': 2.924,
     'sb_bias': 3.824,
     'b_rgate': 8.0,
     'b_igate': 7.991,
     'g_v': 2.86,
     'b_ffn_conv': 3.828}
    for name, (base, spread) in spreads.items():
        noise = np.random.default_rng([zlib.crc32(name.encode()), seed]).standard_normal(out[name].shape)
        drawn = base * np.exp(spread * noise) if base else spread * noise
        out[name] = __import__('jax').numpy.asarray(drawn.astype(out[name].dtype))
    for name, factor in factors.items():
        out[name] = (out[name] * factor).astype(out[name].dtype)
    return out
```

```python
from contextlib import ExitStack

import concourse.bass as bass
from concourse import mybir

F32 = mybir.dt.float32
F32R = mybir.dt.float32r
ACT = mybir.ActivationFunctionType
ALU = mybir.AluOpType

P = 128
D = 1024
KT = D // P
SEQ = 1024
NSEQ, SLEN = 8, 8
NS = NSEQ * SLEN
CH = 364
T = 3 * CH
PAGE, PAGES = 128, 8
HD = 64
FF = 3 * D
FT = FF // P
EPS = 1e-6
ZCAP = 40.0
MASKED = -1.0e30


class Order:

    def __init__(self, eng, sem):
        self.eng, self.sem, self.base, self.k = eng, sem, 0, 0
        self.last = None

    def did(self, inst):
        inst.then_inc(self.sem, 1)
        self.k += 1
        self.last = (self.sem, self.base + self.k)

    def raises(self, inst, sem, value):
        inst.then_inc(sem, 1)
        self.last = (sem, value)

    def after(self):
        self.eng.wait_ge(*self.last)

    def enter(self, i, per):
        self.start, self.per = self.base + self.k, per
        self.base, self.k = self.start + i * per, 0

    def leave(self, trips):
        assert self.k == self.per, (self.k, self.per)
        self.base, self.k = self.start + trips * self.per, 0


class Weights:

    def __init__(self, nc, ctx):
        self.raw = ctx.enter_context(nc.sbuf_tensor("w_raw", [P, 2, D], F32))
        self.hi = ctx.enter_context(nc.sbuf_tensor("w_hi_part", [P, 2, D], F32R))
        self.lo = ctx.enter_context(nc.sbuf_tensor("w_lo_part", [P, 2, D], F32R))
        self.in0 = ctx.enter_context(nc.semaphore("slab_in_even"))
        self.in1 = ctx.enter_context(nc.semaphore("slab_in_odd"))
        self.skew = 0
        self.s_hi = ctx.enter_context(nc.semaphore("slab_hi_ready"))
        self.s_lo = ctx.enter_context(nc.semaphore("slab_lo_ready"))
        self.used = ctx.enter_context(nc.semaphore("slab_used"))

    def load(self, sp, n, par, src):
        sp.wait_ge(self.s_lo, n + 1)
        dst = self.raw[:, par, :]
        if len(src.shape) == 3:
            dst = dst.rearrange("p (k m) -> p k m", k=src.shape[1])
        sp.dma_start(dst, src).then_inc(self.in1 if par else self.in0, 16)

    def split_hi(self, act, n, half, par, free=None, dst=None):
        act.wait_ge(self.in1 if par else self.in0, 16 * (half + 1))
        act.wait_ge(*(free if free else (self.used, n + 1 - self.skew)))
        act.activation(dst if dst is not None else self.hi[:, par, :], self.raw[:, par, :],
                       ACT.Copy).then_inc(self.s_hi, 1)

    def split_hi_at(self, act, n, half, raw, dst, free):
        act.wait_ge(self.in1 if raw else self.in0, 16 * (half + 1))
        act.wait_ge(*free)
        act.activation(dst, self.raw[:, raw, :], ACT.Copy).then_inc(self.s_hi, 1)

    def split_lo_at(self, pool, n, raw, hi, lo):
        pool.wait_ge(self.s_hi, n + 1)
        pool.tensor_tensor(lo, self.raw[:, raw, :], hi.bitcast(F32), ALU.subtract).then_inc(self.s_lo, 1)

    def split_lo(self, pool, n, par, hi=None, dst=None):
        pool.wait_ge(self.s_hi, n + 1)
        pool.tensor_tensor(dst if dst is not None else self.lo[:, par, :], self.raw[:, par, :],
                           (hi if hi is not None else self.hi[:, par, :]).bitcast(F32),
                           ALU.subtract).then_inc(self.s_lo, 1)

    def wait_job(self, eng, n):
        eng.wait_ge(self.used, n + 3 - self.skew)

    def wait_ready(self, pe, n):
        pe.wait_ge(self.s_lo, n + 3)


def chunks(buf):
    return buf.rearrange("p (c n) -> p c n", c=3)


def dense(pe, bank, pairs, x_ready=None):
    last = len(pairs) - 1
    mm = None
    for k, (w_hi, w_lo, x_hi, x_lo) in enumerate(pairs):
        if x_ready:
            x_ready(k)
        for step, (w, x) in enumerate(((w_hi, x_hi), (w_lo, x_hi), (w_hi, x_lo))):
            for c in range(3):
                mm = pe.matmul(bank[:, c, 0:CH], w, x[:, c * CH:(c + 1) * CH],
                               start=(k == 0 and step == 0), stop=(k == last and step == 2))
    return mm


class Core:

    def __init__(self, nc, ctx, dram):
        self.nc, self.dram = nc, dram

        def sb(name, shape, dt=F32):
            return ctx.enter_context(nc.sbuf_tensor(name, shape, dt))

        self.x = sb("x_residual", [P, KT, T])
        self.rb = sb("rms_scale", [P, T])
        self.ident = sb("identity", [P, P])
        self.ones = sb("all_ones", [P, P])
        self.blk = sb("ones_by_head", [P, P])
        self.tri = sb("ones_from_key_on", [P, P])
        self.seen = sb("ones_where_key_before_query", [P, P])
        self.hidden = sb("minus_where_key_not_before_query", [P, P])
        self.par = sb("params", [P, 76])
        self.gate_par = sb("lru_gate_params", [P, 4, 4])
        self.lru_conv0 = sb("lru_conv_state", [P, 4, 24])
        self.lru_h0 = sb("lru_h_state", [P, 4, 8])
        self.bias = sb("stick_bias", [P, 8])
        self.w = Weights(nc, ctx)
        self.ps = ctx.enter_context(nc.psum_tensor("psum_all", [P, 8, 512], F32))
        self.bank_a, self.bank_b = self.ps[:, 0:3, :], self.ps[:, 3:6, :]
        self.phase, self.phase_sems = "", []
        self.slabs = 0

    def sem(self, name):
        self.phase_sems.append(self.nc.alloc_semaphore(name + self.phase))
        return self.phase_sems[-1]

    def free_sems(self):
        self.nc.clear_and_free_semaphores(self.phase_sems)
        self.phase_sems = []
        self.nc.all_engine_barrier()

    def g_mix(self, layer, k):
        return self.par[:, layer * KT + k:layer * KT + k + 1]

    def g_ffn(self, layer, k):
        return self.par[:, 16 + layer * KT + k:16 + layer * KT + k + 1]


def square_slab(weight, col):
    return weight.rearrange("(k p) n -> p k n", p=P)[:, :, bass.ds(col, P)]


def phase_load(core):
    core.phase = "_load"
    nc, dr, w = core.nc, core.dram, core.w
    with ExitStack() as ctx:
        xs = ctx.enter_context(nc.sbuf_tensor("x_rows", [P, 9, D], F32))
        prow = ctx.enter_context(nc.sbuf_tensor("param_rows", [74, P], F32))
        crow = ctx.enter_context(nc.sbuf_tensor("conv_state_rows", [24, 512], F32))
        hrow = ctx.enter_context(nc.sbuf_tensor("h_state_rows", [8, 512], F32))
        sm = ctx.enter_context(nc.sbuf_tensor("softplus_steps", [P, 8, 4], F32))

        def sem(name):
            return core.sem(name)

        x_in = [sem(f"x_rows_in{t}") for t in range(9)]
        small_in, const_ready, tr_done, masks_ready = (sem("params_in"), sem("const_ready"), sem("transposed"),
                                                       sem("masks_ready"))
        act_copied, dve_copied, small_tr, small_copied = (sem("act_copied"), sem("dve_copied"),
                                                           sem("small_transposed"), sem("small_copied"))
        dve_step, exp_ready = sem("dve_step"), sem("exp_ready")
        block = ctx.enter_context(nc.Block())
        groups = [(t, g) for t in range(9) for g in range(2)]

        @block.sync
        def _(sp):
            xp = dr["x_prompt"][0].rearrange("(t p) n -> t p n", p=P)
            for t in range(8):
                sp.dma_start(xs[:, t, :], xp[t]).then_inc(x_in[t], 16)
            sp.dma_start(xs[0:NS, 8, :], dr["x_sample"].rearrange("s t n -> (s t) n")).then_inc(x_in[8], 16)
            rows = [(0, "g_mix"), (16, "g_ffn"), (32, "b_conv_lru"), (36, "w_conv_lru"), (64, "g_v"), (60, "lru_lambda")]
            for at, name in rows:
                a = dr[name].rearrange("a b -> (a b)") if name != "w_conv_lru" and name != "lru_lambda" else \
                    (dr[name].rearrange("a b c -> (a b c)"))
                n = a.shape[0] // P
                sp.dma_start(prow[at:at + n, :], a.rearrange("(r c) -> r c", c=P)).then_inc(small_in, 16)
            for at, name in ((52, "b_rgate"), (56, "b_igate")):
                a = dr[name].rearrange("a b c -> (a b c)")
                sp.dma_start(prow[at:at + 4, :], a.rearrange("(r c) -> r c", c=P)).then_inc(small_in, 16)
            for at, name in ((72, "g_q"), (73, "g_k")):
                for half in range(2):
                    sp.dma_start(prow[at:at + 1, half * HD:(half + 1) * HD], dr[name]).then_inc(small_in, 16)
            sp.dma_start(crow[:, :], dr["state_lru_conv"].rearrange("e s j c -> (e s j) c")).then_inc(small_in, 16)
            sp.dma_start(hrow[:, :], dr["state_lru_h"][0]).then_inc(small_in, 16)
            sp.dma_start(core.bias[:, :], dr["sb_bias"].to_broadcast((P, 8))).then_inc(small_in, 16)
            w_in = dr["w_in_even"][0]
            w.load(sp, 0, 0, square_slab(w_in, 1536))
            w.load(sp, 1, 1, square_slab(w_in, 2048))
            sp.wait_ge(small_in, 16 * 15)

        @block.gpsimd
        def _(pool):
            pool.sem_inc(w.s_lo, 2)
            pool.memset(core.ident[:, :], 0.0).then_inc(const_ready, 1)
            pool.memset(core.ones[:, :], 1.0).then_inc(const_ready, 1)
            pool.memset(core.blk[:, :], 0.0).then_inc(const_ready, 1)
            pool.wait_ge(const_ready, 3)
            pool.affine_select(out=core.ident[:, :], in_=core.ident[:, :], compare_op=ALU.not_equal, fill=1.0,
                               base=0, pattern=[[-1, P]], channel_multiplier=1).then_inc(const_ready, 1)
            pool.affine_select(out=core.tri[:, :], in_=core.ones[:, :], compare_op=ALU.is_ge, fill=0.0,
                               base=0, pattern=[[-1, P]], channel_multiplier=1).then_inc(const_ready, 1)
            pool.affine_select(out=core.seen[:, :], in_=core.ones[:, :], compare_op=ALU.is_gt, fill=0.0,
                               base=0, pattern=[[1, P]], channel_multiplier=-1).then_inc(masks_ready, 1)
            pool.memset(core.hidden[:, :], 0.0).then_inc(masks_ready, 1)
            pool.wait_ge(masks_ready, 2)
            pool.affine_select(out=core.hidden[:, :], in_=core.hidden[:, :], compare_op=ALU.is_gt, fill=MASKED,
                               base=0, pattern=[[1, P]], channel_multiplier=-1).then_inc(masks_ready, 1)
            pool.wait_ge(masks_ready, 3)
            pool.wait_ge(const_ready, 5)
            pool.memset(core.blk[0:HD, 0:HD], 1.0).then_inc(const_ready, 1)
            pool.wait_ge(const_ready, 6)
            pool.memset(core.blk[HD:P, HD:P], 1.0).then_inc(const_ready, 1)
            pool.wait_ge(const_ready, 7)
            w.split_lo(pool, 0, 0)
            w.split_lo(pool, 1, 1)

        @block.tensor
        def _(pe):
            pe.sem_inc(w.used, 2)
            pe.wait_ge(const_ready, 4)
            for n, (t, g) in enumerate(groups):
                rows = P if t < 8 else NS
                if g == 0:
                    pe.wait_ge(x_in[t], 16)
                if n >= 6:
                    pe.wait_ge(act_copied if n % 2 == 0 else dve_copied, (n - 6) // 2 + 1)
                for q in range(4):
                    k = 4 * g + q
                    mm = pe.transpose(core.ps[:, n % 6, q * P:q * P + rows], xs[0:rows, t, k * P:(k + 1) * P],
                                      core.ident[0:rows, 0:rows])
                mm.then_inc(tr_done, 1)
            pe.wait_ge(small_in, 16 * 15)
            pe.transpose(core.ps[:, 6, 0:74], prow[:, :], core.ident[0:74, 0:74])
            for q in range(4):
                pe.transpose(core.ps[:, 6, 80 + 24 * q:104 + 24 * q], crow[:, q * P:(q + 1) * P],
                             core.ident[0:24, 0:24])
                mm = pe.transpose(core.ps[:, 6, 176 + 8 * q:184 + 8 * q], hrow[:, q * P:(q + 1) * P],
                                  core.ident[0:8, 0:8])
            mm.then_inc(small_tr, 1)

        def copy_group(eng, copy, n, sem_done):
            t, g = groups[n]
            rows = P if t < 8 else NS
            eng.wait_ge(tr_done, n + 1)
            copy(core.x[:, 4 * g:4 * g + 4, t * P:t * P + rows],
                 core.ps[:, n % 6, :].rearrange("p (q c) -> p q c", q=4)[:, :, 0:rows]).then_inc(sem_done, 1)

        @block.scalar
        def _(act):
            for n in range(0, 18, 2):
                copy_group(act, act.copy, n, act_copied)
            act.wait_ge(dve_step, 4)
            act.activation(sm[:, 2, :], sm[:, 1, :], ACT.Exp, scale=-1.0).then_inc(exp_ready, 1)
            w.split_hi(act, 0, 0, 0)
            w.split_hi(act, 1, 0, 1)

        @block.vector
        def _(dve):
            o = Order(dve, dve_step)
            o.did(dve.memset(core.x[:, :, SEQ + NS:T], 0.0))
            for n in range(1, 18, 2):
                copy_group(dve, dve.tensor_copy, n, dve_copied)
            dve.wait_ge(small_tr, 1)
            o.did(dve.tensor_copy(core.par[:, 0:74], core.ps[:, 6, 0:74]))
            dve.tensor_copy(core.lru_conv0[:, :, :], core.ps[:, 6, 80:176].rearrange("p (q c) -> p q c", q=4)
                            ).then_inc(small_copied, 1)
            dve.tensor_copy(core.lru_h0[:, :, :], core.ps[:, 6, 176:208].rearrange("p (q c) -> p q c", q=4)
                            ).then_inc(small_copied, 1)
            lam = core.par[:, 60:64]
            y, ay, x, s, s2, p = (sm[:, k, :] for k in (0, 1, 2, 3, 4, 5))
            o.after()
            o.did(dve.tensor_scalar(y, lam, -1.0, None, ALU.mult))
            o.after()
            o.did(dve.tensor_tensor(ay, y, lam, ALU.max))
            dve.wait_ge(exp_ready, 1)
            o.did(dve.tensor_scalar(s, x, 2.0, None, ALU.add))
            o.after()
            o.did(dve.reciprocal(s2, s))
            o.after()
            o.did(dve.tensor_tensor(s, x, s2, ALU.mult))
            o.after()
            o.did(dve.tensor_tensor(s2, s, s, ALU.mult))
            o.after()
            o.did(dve.tensor_scalar(p, s2, 1.0 / 17, 1.0 / 15, ALU.mult, ALU.add))
            for c in (13, 11, 9, 7, 5, 3, 1):
                o.after()
                o.did(dve.tensor_tensor(p, p, s2, ALU.mult))
                o.after()
                o.did(dve.tensor_scalar(p, p, 1.0 / c, None, ALU.add))
            o.after()
            o.did(dve.scalar_tensor_tensor(p, p, 2.0, s, ALU.mult, ALU.mult))
            o.after()
            o.did(dve.scalar_tensor_tensor(p, y, 0.0, p, ALU.max, ALU.add))
            o.after()
            o.did(dve.tensor_scalar(core.gate_par[:, :, 2], p, -8.0, None, ALU.mult))
            o.did(dve.tensor_scalar(core.gate_par[:, :, 3], p, 8.0, None, ALU.mult))
            o.did(dve.tensor_copy(core.gate_par[:, :, 0], core.par[:, 52:56]))
            o.did(dve.tensor_copy(core.gate_par[:, :, 1], core.par[:, 56:60]))


class Norm:

    def __init__(self, core, ctx, tag, act_hi, act_lo, sums, squares, gain):
        self.core, self.hi, self.lo, self.sums, self.sq, self.gain = core, act_hi, act_lo, sums, squares, gain

        def sem(name):
            return core.sem(name + tag)

        self.s_hi, self.s_lo, self.s_sq = sem("xn_hi"), sem("xn_lo"), sem("squares")
        self.s_sum, self.s_mm, self.s_root, self.s_rb = sem("sq_sums"), sem("sum_mm"), sem("roots"), sem("rb_ready")

    def split_act(self, act):
        for k in range(KT):
            act.activation(self.hi[:, k, :], self.core.x[:, k, :], ACT.Copy,
                           scale=self.gain(k)).then_inc(self.s_hi, 1)

    def squares_act(self, act):
        for k in range(KT):
            if k >= 3:
                act.wait_ge(self.s_sum, k - 2)
            dst = self.sums[:, :] if k == 0 else self.sq[k % 2]
            act.activation(dst, self.core.x[:, k, :], ACT.Square).then_inc(self.s_sq, 1)

    def split_dve(self, dve):
        for k in range(KT):
            dve.wait_ge(self.s_hi, k + 1)
            dve.scalar_tensor_tensor(self.lo[:, k, :], self.core.x[:, k, :], self.gain(k),
                                     self.hi[:, k, :].bitcast(F32), ALU.mult, ALU.subtract).then_inc(self.s_lo, 1)

    def sums_dve(self, dve):
        for k in range(1, KT):
            dve.wait_ge(self.s_sq, k + 1)
            if k > 1:
                dve.wait_ge(self.s_sum, k - 1)
            dve.tensor_tensor(self.sums[:, :], self.sums[:, :], self.sq[k % 2], ALU.add).then_inc(self.s_sum, 1)

    def sums_pe(self, pe):
        pe.wait_ge(self.s_sum, KT - 1)
        for c in range(3):
            if c == 2:
                pe.wait_ge(self.s_root, 1)
            pe.matmul(self.core.ps[:, 6 + c % 2, 0:CH], self.core.ones[:, :], self.sums[:, c * CH:(c + 1) * CH],
                      start=True, stop=True).then_inc(self.s_mm, 1)

    def roots_act(self, act):
        act.preload_act_table_set("natural_log_exp_and_others")
        for c in range(3):
            act.wait_ge(self.s_mm, c + 1)
            act.activation(self.core.rb[:, c * CH:(c + 1) * CH], self.core.ps[:, 6 + c % 2, 0:CH], ACT.Ln,
                           scale=1.0 / D, bias=EPS).then_inc(self.s_root, 1)
        act.wait_ge(self.s_root, 3)
        act.activation(self.core.rb[:, :], self.core.rb[:, :], ACT.Exp, scale=-0.5).then_inc(self.s_rb, 1)

    def scale_dve(self, dve):
        dve.wait_ge(self.s_rb, 1)


def phase_lru(core, act_hi, act_lo, mix):
    core.phase = "_lru"
    nc, dr, w = core.nc, core.dram, core.w
    n0 = core.slabs
    with ExitStack() as ctx:
        def sb(name, shape, dt=F32):
            return ctx.enter_context(nc.sbuf_tensor(name, shape, dt))

        def sem(name):
            return core.sem(name)

        xb = sb("xb_padded", [P, 4 + T])
        xc, rt, it, at, th, gb = (sb(n, [P, T]) for n in ("xc_then_h", "r_gate", "i_gate", "a_decay", "one_minus_a2",
                                                          "gelu_gate"))
        xs = sb("xb_sample", [P, NSEQ, 3 + SLEN])
        hf = sb("h0_term", [P, NSEQ])
        bd = sb("gate_weights", [P, 2, P])
        gp = sb("tile_gate_params", [P, 1, 4])
        pk = sb("state_columns", [P, 4, 36])
        st = sb("state_rows", [36, 512])
        norm = Norm(core, ctx, "_lru", act_hi, act_lo, at, [th[:, :], gb[:, :]], lambda k: core.g_mix(0, k))
        evac, xc_ready, gate_mm, gate_read = sem("evac"), sem("xc_ready"), sem("gate_mm"), sem("gate_read")
        bd_in, bd_zero, a_ready, th_ready, m_ready, root_ready = (sem("bd_in"), sem("bd_zero"), sem("a_ready"),
                                                                  sem("th_ready"), sem("m_ready"), sem("root_ready"))
        gelu_ready, h_done, dve_step = sem("gelu_ready"), sem("h_done"), sem("dve_step")
        pk_tr, st_ready, stored, act_step = sem("pk_tr"), sem("st_ready"), sem("stored"), sem("act_step")
        block = ctx.enter_context(nc.Block())
        w_in = dr["w_in_even"][0]

        @block.sync
        def _(sp):
            def gates(j):
                sp.wait_ge(gate_mm, 6 * j + 1)
                for g, name in enumerate(("w_rgate", "w_igate")):
                    blocks = dr[name][0].rearrange("h c d -> (h c) d")
                    for b in range(2):
                        sp.dma_start(bd[b * HD:(b + 1) * HD, g, b * HD:(b + 1) * HD],
                                     blocks[bass.ds(j * P + b * HD, HD), :]).then_inc(bd_in, 16)

            sp.wait_ge(bd_zero, 1)
            with sp.Fori(0, 3) as i:
                gates(i)
                w.load(sp, n0 + 2 * i + 2, 0, square_slab(w_in, (i + 1) * P + 1536))
                w.load(sp, n0 + 2 * i + 3, 1, square_slab(w_in, (i + 1) * P + 2048))
            gates(3)
            w.load(sp, n0 + 8, 0, square_slab(w_in, 0))
            w.load(sp, n0 + 9, 1, square_slab(w_in, 512))
            sp.wait_ge(st_ready, 1)
            sp.dma_start(dr["lru_h_prompt"][0], st[0:1, :]).then_inc(stored, 16)
            sp.dma_start(dr["lru_h_sample"][0], st[1:9, :]).then_inc(stored, 16)
            sp.dma_start(dr["lru_conv_prompt"][0, 0], st[9:12, :]).then_inc(stored, 16)
            sp.dma_start(dr["lru_conv_sample"][0].rearrange("s j c -> (s j) c"), st[12:36, :]).then_inc(stored, 16)
            sp.wait_ge(stored, 64)

        @block.gpsimd
        def _(pool):
            pool.memset(bd[:, :, :], 0.0).then_inc(bd_zero, 1)
            with pool.Fori(0, 4) as i:
                w.split_lo(pool, n0 + 2 * i + 2, 0)
                w.split_lo(pool, n0 + 2 * i + 3, 1)

        @block.tensor
        def _(pe):
            pe.sem_inc(gate_mm, 1)

            def job(i, par, bank, x_ready=None):
                w.wait_ready(pe, n0 + 2 * i + par)
                pe.wait_ge(evac, 2 * i + par + 1)
                dense(pe, bank, [(w.hi[:, par, k * P:(k + 1) * P], w.lo[:, par, k * P:(k + 1) * P],
                                  act_hi[:, k, :], act_lo[:, k, :]) for k in range(KT)], x_ready).then_inc(w.used, 1)

            def gates(i):
                pe.wait_ge(xc_ready, i + 1)
                pe.wait_ge(bd_in, 64 * i + 64)
                for c in range(3):
                    for g in range(2):
                        pe.wait_ge(gate_read, 6 * i + 2 * c + g + 1)
                        pe.matmul(core.ps[:, 6 + g, 0:CH], bd[:, g, :], xc[:, c * CH:(c + 1) * CH],
                                  start=True, stop=True).then_inc(gate_mm, 1)

            job(0, 0, core.bank_a, lambda k: pe.wait_ge(norm.s_lo, k + 1))
            job(0, 1, core.bank_b, lambda k: norm.sums_pe(pe) if k == KT // 2 else None)
            gates(0)
            with pe.Fori(1, 4) as i:
                job(i, 0, core.bank_a)
                job(i, 1, core.bank_b)
                gates(i)
            pe.wait_ge(h_done, 5)
            pe.wait_ge(gate_read, 26)
            for j in range(4):
                mm = pe.transpose(core.ps[0:36, 6, j * P:(j + 1) * P], pk[:, j, :], core.ident[:, :])
            mm.then_inc(pk_tr, 1)

        @block.scalar
        def _(act):
            norm.split_act(act)
            norm.squares_act(act)
            norm.roots_act(act)
            act.sem_inc(gate_read, 2)
            o = Order(act, act_step)
            with act.Fori(0, 4) as i:
                o.enter(i, 0)
                w.split_hi(act, n0 + 2 * i + 2, n0 // 2 + i + 1, 0)
                w.split_hi(act, n0 + 2 * i + 3, n0 // 2 + i + 1, 1)
                for c in range(3):
                    for g, (dst, col) in enumerate(((rt, 0), (it, 1))):
                        act.wait_ge(gate_mm, 6 * i + 2 * c + g + 2)
                        act.activation(dst[:, c * CH:(c + 1) * CH], core.ps[:, 6 + g, 0:CH], ACT.Sigmoid,
                                       bias=gp[:, 0, col:col + 1]).then_inc(gate_read, 1)
                act.wait_ge(gate_read, 6 * i + 8)
                act.activation(at[:, :], rt[:, :], ACT.Exp, scale=gp[:, 0, 2:3]
                               ).then_inc(a_ready, 1)
                act.activation(th[:, :], rt[:, :], ACT.Tanh, scale=gp[:, 0, 3:4]
                               ).then_inc(th_ready, 1)
                act.wait_ge(m_ready, i + 1)
                act.activation(rt[:, :], rt[:, :], ACT.Sqrt).then_inc(root_ready, 1)
                act.wait_ge(evac, 2 * i + 4)
                act.activation(gb[:, :], gb[:, :], ACT.Gelu_apprx_tanh).then_inc(gelu_ready, 1)
                o.leave(4)
            act.wait_ge(pk_tr, 1)
            act.copy(st[:, :], core.ps[0:36, 6, :]).then_inc(st_ready, 1)

        @block.vector
        def _(dve):
            o = Order(dve, dve_step)
            dve.sem_inc(evac, 2)
            dve.sem_inc(h_done, 1)
            norm.split_dve(dve)
            norm.sums_dve(dve)
            o.did(dve.memset(xb[:, 0:3], 0.0))
            o.after()
            norm.scale_dve(dve)
            with dve.Fori(0, 4) as i:
                o.enter(i, 21)
                w.wait_job(dve, n0 + 2 * i)
                dve.wait_ge(h_done, i + 1)
                o.raises(dve.tensor_tensor(chunks(xb[:, 3:3 + T]), core.bank_a[:, :, 0:CH], chunks(core.rb[:, :]),
                                           ALU.mult), evac, 2 * i + 3)

                def tap(j):
                    return core.par[:, bass.ds(i + (36 + 4 * j), 1)]

                bias = core.par[:, bass.ds(i + 32, 1)]
                o.after()
                o.did(dve.tensor_scalar(xc[:, :], xb[:, 3:3 + T], tap(3), bias, ALU.mult, ALU.add))
                for j in (2, 1, 0):
                    o.after()
                    o.did(dve.scalar_tensor_tensor(xc[:, :], xb[:, j:j + T], tap(j), xc[:, :], ALU.mult, ALU.add))
                o.did(dve.tensor_copy(xs[:, :, 0:3], core.lru_conv0[:, bass.ds(i, 1), :]
                                      .rearrange("p o (s j) -> p (o s) j", j=3)))
                o.did(dve.tensor_copy(xs[:, :, 3:3 + SLEN],
                                      xb[:, 3 + SEQ:3 + SEQ + NS].rearrange("p (s t) -> p s t", t=SLEN)))
                o.did(dve.tensor_copy(gp[:, :, :], core.gate_par[:, bass.ds(i, 1), :]))
                xcs = xc[:, SEQ:SEQ + NS].rearrange("p (s t) -> p s t", t=SLEN)
                o.after()
                o.did(dve.tensor_scalar(xcs, xs[:, :, 3:3 + SLEN], tap(3), bias, ALU.mult, ALU.add))
                for j in (2, 1, 0):
                    o.after()
                    step = dve.scalar_tensor_tensor(xcs, xs[:, :, j:j + SLEN], tap(j), xcs, ALU.mult, ALU.add)
                    if j:
                        o.did(step)
                    else:
                        o.raises(step, xc_ready, i + 1)
                o.did(dve.tensor_copy(pk[:, bass.ds(i, 1), 9:12], xb[:, 3 + SEQ - 3:3 + SEQ]))
                o.did(dve.tensor_copy(pk[:, bass.ds(i, 1), 12:36].rearrange("p o (s j) -> p (o s) j", j=3),
                                      xs[:, :, SLEN:3 + SLEN]))
                w.wait_job(dve, n0 + 2 * i + 1)
                o.raises(dve.tensor_tensor(chunks(gb[:, :]), core.bank_b[:, :, 0:CH], chunks(core.rb[:, :]),
                                           ALU.mult), evac, 2 * i + 4)
                dve.wait_ge(th_ready, i + 1)
                o.did(dve.tensor_tensor(rt[:, :], at[:, :], at[:, :], ALU.mult))
                o.after()
                o.raises(dve.scalar_tensor_tensor(rt[:, :], rt[:, :], 1.0, th[:, :], ALU.add, ALU.mult),
                         m_ready, i + 1)
                o.did(dve.tensor_tensor(it[:, :], it[:, :], xc[:, :], ALU.mult))
                dve.wait_ge(root_ready, i + 1)
                o.after()
                o.did(dve.tensor_tensor(it[:, :], it[:, :], rt[:, :], ALU.mult))
                a0 = at[:, SEQ:SEQ + NS].rearrange("p (s t) -> p s t", t=SLEN)[:, :, 0]
                u0 = it[:, SEQ:SEQ + NS].rearrange("p (s t) -> p s t", t=SLEN)[:, :, 0]
                o.did(dve.tensor_tensor(hf[:, :], a0, core.lru_h0[:, bass.ds(i, 1), :]
                                        .rearrange("p o s -> p (o s)"), ALU.mult))
                o.after()
                o.did(dve.tensor_tensor(u0, u0, hf[:, :], ALU.add))
                o.after()
                o.did(dve.memset(a0, 0.0))
                o.after()
                o.did(dve.tensor_tensor_scan(xc[:, :], at[:, :], it[:, :], 0.0, ALU.mult, ALU.add))
                o.after()
                o.did(dve.tensor_copy(pk[:, bass.ds(i, 1), 0:1], xc[:, SEQ - 1:SEQ]))
                hs = xc[:, SEQ:SEQ + NS].rearrange("p (s t) -> p s t", t=SLEN)[:, :, SLEN - 1]
                o.did(dve.tensor_copy(pk[:, bass.ds(i, 1), 1:9].rearrange("p o s -> p (o s)"), hs))
                o.after()
                dve.wait_ge(gelu_ready, i + 1)
                o.raises(dve.tensor_tensor(mix[:, bass.ds(i + 4, 1), :].rearrange("p o t -> p (o t)"), xc[:, :],
                                           gb[:, :], ALU.mult), h_done, i + 2)
                o.leave(4)
    core.slabs += 8



def attention_units():
    units = []
    for head in range(2):
        for half in (1, 0):
            top = 4 * half + 3
            for kb in range(top, -1, -1):
                q0 = max(kb * P, half * 512)
                units.append(dict(head=head, half=half, kb=kb, q0=q0, off=q0 - half * 512,
                                  diag=kb * P >= half * 512, first=kb == top, last=kb == 0,
                                  group=2 * head + 1 - half))
    diags = keeps = 0
    for u in units:
        diags += u["diag"]
        keeps += not u["last"]
        u["diags"], u["keeps"] = diags, keeps
    return units


def phase_attention(core, act_hi, act_lo, mix, k_sample):
    core.phase = "_prompt"
    nc, dr, w = core.nc, core.dram, core.w
    n0 = core.slabs
    units = attention_units()
    NU, ND, NK = len(units), units[-1]["diags"], units[-1]["keeps"]
    with ExitStack() as ctx:
        def sb(name, shape, dt=F32):
            return ctx.enter_context(nc.sbuf_tensor(name, shape, dt))

        def sem(name):
            return core.sem(name)

        qt, kt, sq, rq = (sb(n, [P, T]) for n in ("q_pair", "k_pair", "qk_squares", "qk_scale"))
        vt = sq
        later = [rq[:, 0:512], rq[:, 512:1024], sq[:, 0:512]]
        vtok = sb("v_tokens", [P, 9, P])
        kst = sb("k_rows_out", [P, 9, P])
        zs = sb("logits_then_weights", [P, 4, 512])
        sp2 = sb("softplus", [P, 2, 512])
        es = [sp2[:, 0, :], sp2[:, 1, :], sq[:, 512:1024]]
        evac, sq_ready, nrm_mm, xy_read, q_ready, k_ready = (sem(n) for n in (
            "evac", "sq_ready", "nrm_mm", "spare_read", "q_ready", "k_ready"))
        tr_done, kst_ready, kst_free, kst_out, v_ready, v_out, v_free = (sem(n) for n in (
            "transposed", "kst_ready", "kst_free", "kst_out", "v_ready", "v_out", "v_free"))
        qk_done, z_read, e_ready, ln_ready, sp_ready, s_done, d_ready, w_ready, pv_done, o_out = (sem(n) for n in (
            "qk_done", "z_read", "e_ready", "ln_ready", "sp_ready", "s_done", "d_ready", "w_ready", "pv_done",
            "o_out"))
        root_ready = sem("root_ready")
        sp_masked, d_masked, later_ready = sem("sp_masked"), sem("d_masked"), sem("later_ready")
        dve_step, act_step, pool_step = sem("dve_step"), sem("act_step"), sem("pool_step")
        block = ctx.enter_context(nc.Block())
        w_in, w_out = dr["w_in_even"][0], dr["w_out_even"][0]

        @block.sync
        def _(sp):
            sp.sem_inc(kst_free, 1)
            sp.sem_inc(v_free, 1)
            k_rows = dr["k_prompt"][0, 0].rearrange("(t p) h d -> p t (h d)", p=P)
            v_rows = dr["v_prompt"][0, 0].rearrange("(t p) h d -> p t (h d)", p=P)
            k_new = dr["k_sample"][0].rearrange("s t h d -> (s t) (h d)")
            v_new = dr["v_sample"][0].rearrange("s t h d -> (s t) (h d)")
            for j in range(4):
                c = slice(j * P, (j + 1) * P)
                w.load(sp, n0 + 3 * j + 2, (3 * j + 2) % 2, square_slab(w_in, 1024 + j * P))
                for r in range(2):
                    src = square_slab(w_in, 512 * r + (j + 1) * P) if j < 3 else square_slab(w_out, r * P)
                    w.load(sp, n0 + 3 * j + 3 + r, (3 * j + 3 + r) % 2, src)
                sp.wait_ge(v_ready, j + 1)
                sp.dma_start(v_rows[:, :, c], vtok[:, 0:8, :]).then_inc(v_out, 16)
                sp.dma_start(v_new[:, c], vtok[0:NS, 8, :]).then_inc(v_out, 16)
                sp.wait_ge(kst_ready, j + 1)
                sp.dma_start(k_rows[:, :, c], kst[:, 0:8, :]).then_inc(kst_out, 16)
                sp.dma_start(k_new[:, c], kst[0:NS, 8, :]).then_inc(kst_out, 16)
                sp.wait_ge(kst_out, 32 * (j + 1))
                sp.sem_inc(kst_free, 1)
                sp.wait_ge(v_out, 32 * (j + 1))
                sp.sem_inc(v_free, 1)

        def run(*stages):
            for n in range(-2, NU + 3):
                for stage, ahead in zip(stages[::2], stages[1::2]):
                    if 0 <= n + ahead < NU:
                        stage(n + ahead)

        def pairs(eng, body):
            with eng.Fori(0, 2) as i:
                for jj in range(2):
                    body(i, jj, 2 * i + jj)

        @block.tensor
        def _(pe):
            pe.sem_inc(pv_done, 4)
            pe.sem_inc(s_done, 3)

            def body(i, jj, p):
                def job(r, between=None):
                    s = 3 * jj + r
                    n = 6 * i + s
                    w.wait_ready(pe, n0 + n)
                    pe.wait_ge(evac, n + 1)
                    dense(pe, (core.bank_a, core.bank_b)[s % 2],
                          [(w.hi[:, s % 2, k * P:(k + 1) * P], w.lo[:, s % 2, k * P:(k + 1) * P],
                            act_hi[:, k, :], act_lo[:, k, :]) for k in range(KT)],
                          lambda k: between(r - 1) if between and k == KT // 2 else None).then_inc(w.used, 1)

                def norm_sums(r):
                    pe.wait_ge(sq_ready, 2 * p + r + 1)
                    for c in range(3):
                        use = 3 * r + c
                        pe.wait_ge(xy_read, 12 * p + use + 1)
                        pe.matmul(core.ps[:, 6 + use % 2, 0:CH], core.blk[:, :], sq[:, c * CH:(c + 1) * CH],
                                  start=True, stop=True).then_inc(nrm_mm, 1)

                def to_rows(src, first_use):
                    for g in range(3):
                        use = first_use + g
                        pe.wait_ge(xy_read, 12 * p + use + 1)
                        for q in range(4 if g < 2 else 1):
                            t = 4 * g + q
                            m = P if t < 8 else T - SEQ
                            mm = pe.transpose(core.ps[0:m, 6 + use % 2, q * P:(q + 1) * P],
                                              src[:, t * P:t * P + m], core.ident[:, :])
                        mm.then_inc(tr_done, 1)

                pe.wait_ge(o_out, 4 * p + 2)
                job(0)
                job(1, norm_sums)
                job(2, norm_sums)

                def logits(n):
                    u = units[n]
                    b = HD * u["head"]
                    pe.wait_ge(z_read, NU * p + n + 1)
                    pe.matmul(core.ps[:, n % 2, u["off"]:512], kt[b:b + HD, u["kb"] * P:(u["kb"] + 1) * P],
                              qt[b:b + HD, u["q0"]:512 * (u["half"] + 1)], start=True, stop=True
                              ).then_inc(qk_done, 1)

                def sums(n):
                    u = units[n]
                    pe.wait_ge(d_ready, NU * p + n + 1)
                    if u["diag"]:
                        pe.wait_ge(sp_masked, ND * p + u["diags"])
                    else:
                        pe.wait_ge(sp_ready, NU * p + n + 1)
                    mm = pe.matmul(core.ps[:, 2 + n % 2, u["off"]:512], core.tri[:, :],
                                   es[n % 3][:, u["off"]:512], start=True, stop=u["first"])
                    if not u["first"]:
                        prev = units[n - 1]
                        pe.wait_ge(later_ready, NK * p + prev["keeps"])
                        mm = pe.matmul(core.ps[:, 2 + n % 2, prev["off"]:512], core.ones[:, :],
                                       later[(n - 1) % 3][:, prev["off"]:512], start=False, stop=True)
                    mm.then_inc(s_done, 1)

                def values(n):
                    u = units[n]
                    b = HD * u["head"]
                    if u["first"]:
                        pe.wait_ge(o_out, 4 * p + u["group"] + 1)
                    pe.wait_ge(w_ready, NU * p + n + 1)
                    pe.matmul(core.ps[b:b + HD, 4 + u["group"] % 2, u["off"]:512], vtok[:, u["kb"], b:b + HD],
                              zs[:, n % 4, u["off"]:512], start=u["first"], stop=u["last"],
                              skip_group_check=True).then_inc(pv_done, 1)

                pe.wait_ge(k_ready, p + 1)
                pe.wait_ge(evac, 3 * p + 5)
                logits(0)
                logits(1)
                to_rows(vt, 6)
                to_rows(kt, 9)
                run(lambda n: logits(n) if n > 1 else None, 2, sums, 0, values, -1)

            pairs(pe, body)

        @block.scalar
        def _(act):
            act.sem_inc(xy_read, 2)
            o = Order(act, act_step)

            def body(i, jj, p):
                def split(r):
                    s = 3 * jj + r
                    w.split_hi(act, n0 + 6 * i + s, n0 // 2 + 3 * i + s // 2, s % 2)

                def inverse_roots(r):
                    for c in range(3):
                        act.wait_ge(nrm_mm, 6 * p + 3 * r + c + 1)
                        act.activation(rq[:, c * CH:(c + 1) * CH], core.ps[:, 6 + (3 * r + c) % 2, 0:CH], ACT.Ln,
                                       scale=1.0 / HD, bias=EPS).then_inc(xy_read, 1)
                    act.wait_ge(xy_read, 12 * p + 3 * r + 5)
                    act.activation(rq[:, :], rq[:, :], ACT.Exp, scale=-0.5).then_inc(root_ready, 1)

                split(2)
                act.wait_ge(evac, 3 * p + 3)
                act.activation(sq[:, :], qt[:, :], ACT.Square).then_inc(sq_ready, 1)
                inverse_roots(0)
                split(3)
                act.wait_ge(evac, 3 * p + 4)
                act.activation(sq[:, :], kt[:, :], ACT.Square).then_inc(sq_ready, 1)
                act.wait_ge(q_ready, p + 1)
                inverse_roots(1)
                split(4)
                def rows_of_v():
                    act.wait_ge(v_free, p + 1)
                    for g in range(3):
                        act.wait_ge(tr_done, 6 * p + g + 1)
                        m, n = (P, 4) if g < 2 else (NS, 1)
                        act.activation(vtok[0:m, 4 * g:4 * g + n, :],
                                       core.ps[0:m, 6 + g % 2, 0:n * P].rearrange("p (t c) -> p t c", c=P),
                                       ACT.Copy).then_inc(xy_read, 1)
                    act.wait_ge(xy_read, 12 * p + 11)
                    act.sem_inc(v_ready, 1)

                def rows_of_k():
                    act.wait_ge(kst_free, p + 1)
                    for g in range(3):
                        act.wait_ge(tr_done, 6 * p + g + 4)
                        m, n = (P, 4) if g < 2 else (NS, 1)
                        act.activation(kst[0:m, 4 * g:4 * g + n, :],
                                       core.ps[0:m, 6 + (9 + g) % 2, 0:n * P].rearrange("p (t c) -> p t c", c=P),
                                       ACT.Copy).then_inc(xy_read, 1)
                    act.wait_ge(xy_read, 12 * p + 14)
                    act.sem_inc(kst_ready, 1)

                def soft(n):
                    e = es[n % 3][:, units[n]["off"]:512]
                    act.wait_ge(e_ready, NU * p + n + 1)
                    o.did(act.activation(e, e, ACT.Exp))
                    o.after()
                    act.activation(e, e, ACT.Ln, bias=1.0).then_inc(ln_ready, 1)

                def weights(n):
                    u = units[n]
                    z = zs[:, n % 4, u["off"]:512]
                    if u["diag"]:
                        act.wait_ge(d_masked, ND * p + u["diags"])
                    else:
                        act.wait_ge(d_ready, NU * p + n + 3)
                    act.activation(z, z, ACT.Exp).then_inc(w_ready, 1)

                act.preload_act_table_set("natural_log_exp_and_others")
                soft(0)
                rows_of_v()
                soft(1)
                rows_of_k()
                run(weights, -1, lambda n: soft(n) if n > 1 else None, 2)

            with act.Fori(0, 2) as i:
                o.enter(i, 2 * NU)
                for jj in range(2):
                    body(i, jj, 2 * i + jj)
                o.leave(2)

        @block.gpsimd
        def _(pool):
            o = Order(pool, pool_step)

            def body(i, jj, p):
                for r in (2, 3, 4):
                    s = 3 * jj + r
                    w.split_lo(pool, n0 + 6 * i + s, s % 2)

                def hide(n):
                    u = units[n]
                    if u["diag"]:
                        z = zs[:, n % 4, u["off"]:u["off"] + P]
                        pool.wait_ge(d_ready, NU * p + n + 3)
                        pool.tensor_tensor(z, z, core.hidden[:, :], ALU.add).then_inc(d_masked, 1)

                def running(n):
                    u = units[n]
                    e = es[n % 3]
                    lo, hi = u["off"], u["off"] + P
                    pool.wait_ge(sp_ready, NU * p + n + 1)
                    if u["diag"]:
                        pool.tensor_tensor(e[:, lo:hi], e[:, lo:hi], core.seen[:, :], ALU.mult).then_inc(sp_masked, 1)
                        pool.wait_ge(sp_masked, ND * p + u["diags"])
                    if u["last"]:
                        return
                    if n >= 1:
                        pool.wait_ge(s_done, NU * p + n + 2)
                    if u["diag"]:
                        step = pool.tensor_tensor(later[n % 3][:, lo:hi], e[:, lo:hi], core.ones[:, :], ALU.mult)
                        if u["first"]:
                            step.then_inc(later_ready, 1)
                        else:
                            o.did(step)
                    if not u["first"]:
                        at = units[n - 1]["off"]
                        pool.wait_ge(later_ready, NK * p + units[n - 1]["keeps"])
                        if u["diag"]:
                            o.after()
                        pool.tensor_tensor(later[n % 3][:, at:512], later[(n - 1) % 3][:, at:512], e[:, at:512],
                                           ALU.add).then_inc(later_ready, 1)

                run(hide, -1, running, 1)

            per_pair = sum(u["diag"] and not u["first"] and not u["last"] for u in units)
            with pool.Fori(0, 2) as i:
                o.enter(i, 2 * per_pair)
                for jj in range(2):
                    body(i, jj, 2 * i + jj)
                o.leave(2)

        @block.vector
        def _(dve):
            dve.sem_inc(evac, 2)
            dve.sem_inc(z_read, 2)
            dve.sem_inc(d_ready, 2)
            dve.sem_inc(o_out, 2)
            o = Order(dve, dve_step)
            o.did(dve.memset(mix[:, 0:4, SEQ + NS:T], 0.0))
            o.after()

            def body(i, jj, p):
                def evacuate(r, dst):
                    w.wait_job(dve, n0 + 6 * i + 3 * jj + r)
                    dve.tensor_tensor(chunks(dst[:, :]), (core.bank_a, core.bank_b)[(3 * jj + r) % 2][:, :, 0:CH],
                                      chunks(core.rb[:, :]), ALU.mult).then_inc(evac, 1)

                def normalize(r, buf, col, done):
                    dve.wait_ge(root_ready, 2 * p + r + 1)
                    dve.scalar_tensor_tensor(buf[:, :], buf[:, :], core.par[:, col:col + 1], rq[:, :],
                                             ALU.mult, ALU.mult).then_inc(done, 1)

                dve.wait_ge(o_out, 4 * p + 2)
                evacuate(0, qt)
                dve.wait_ge(evac, 3 * p + 3)
                normalize(0, qt, 72, q_ready)
                evacuate(1, kt)
                dve.wait_ge(evac, 3 * p + 4)
                normalize(1, kt, 73, k_ready)
                dve.wait_ge(nrm_mm, 6 * p + 6)
                evacuate(2, vt)
                dve.wait_ge(k_ready, p + 1)
                o.did(dve.tensor_scalar(mix[:, bass.ds(p, 1), SEQ:SEQ + NS].rearrange("p o t -> p (o t)"),
                                        qt[:, SEQ:SEQ + NS], 1.0, None, ALU.mult))
                o.did(dve.tensor_scalar(k_sample[:, bass.ds(p, 1), :].rearrange("p o t -> p (o t)"),
                                        kt[:, SEQ:SEQ + NS], 1.0, None, ALU.mult))

                def logits(n):
                    u = units[n]
                    z, e = zs[:, n % 4, u["off"]:512], es[n % 3][:, u["off"]:512]
                    dve.wait_ge(pv_done, NU * p + n + 1)
                    dve.wait_ge(qk_done, NU * p + n + 1)
                    dve.tensor_scalar(z, core.ps[:, n % 2, u["off"]:512], 0.125,
                                      core.bias[:, bass.ds(4 * i + 2 * jj + u["head"], 1)], ALU.mult, ALU.add
                                      ).then_inc(z_read, 1)
                    if n >= 3:
                        dve.wait_ge(later_ready, NK * p + units[n - 3]["keeps"])
                    dve.wait_ge(s_done, NU * p + n + 1)
                    dve.wait_ge(z_read, NU * p + n + 3)
                    dve.tensor_scalar(e, z, ZCAP, None, ALU.min).then_inc(e_ready, 1)

                def softplus(n):
                    u = units[n]
                    z, e = zs[:, n % 4, u["off"]:512], es[n % 3][:, u["off"]:512]
                    dve.wait_ge(ln_ready, NU * p + n + 1)
                    dve.tensor_tensor(e, z, e, ALU.max).then_inc(sp_ready, 1)

                def differences(n):
                    u = units[n]
                    z = zs[:, n % 4, u["off"]:512]
                    dve.wait_ge(s_done, NU * p + n + 4)
                    dve.tensor_tensor(z, z, core.ps[:, 2 + n % 2, u["off"]:512], ALU.subtract).then_inc(d_ready, 1)

                def out(n):
                    u = units[n]
                    if not u["last"]:
                        return
                    b = HD * u["head"]
                    dve.wait_ge(pv_done, NU * p + n + 5)
                    dve.tensor_scalar(mix[b:b + HD, bass.ds(p, 1), 512 * u["half"]:512 * (u["half"] + 1)]
                                      .rearrange("p o t -> p (o t)"), core.ps[b:b + HD, 4 + u["group"] % 2, :], 1.0,
                                      None, ALU.mult).then_inc(o_out, 1)

                run(differences, -1, softplus, 1, logits, 2, out, -2)

            with dve.Fori(0, 2) as i:
                o.enter(i, 4)
                for jj in range(2):
                    body(i, jj, 2 * i + jj)
                o.leave(2)
    core.slabs += 12



def phase_sample_attention(core, mix, k_sample):
    core.phase = "_sample"
    nc, dr = core.nc, core.dram
    with ExitStack() as ctx:
        def sb(name, shape, dt=F32):
            return ctx.enter_context(nc.sbuf_tensor(name, shape, dt))

        def sem(name):
            return core.sem(name)

        table = sb("page_table", [1, NSEQ * PAGES], mybir.dt.int64)
        kp, vp = sb("k_pages", [P, 2, PAGES, 512]), sb("v_pages", [P, 2, PAGES, 512])
        ktr = sb("k_pages_transposed", [P, 4, PAGES * PAGE])
        zs, es, suf = sb("s_logits", [P, 2, 8, 64]), sb("s_softplus", [P, 2, 8, 64]), sb("later_pages", [P, 7, 64])
        qd = sb("q_by_head", [P, 4, NSEQ, 16])
        brow = sb("bias_row", [P, 8, 8])
        same = sb("same_sequence_and_before", [NS, NS])
        gone = sb("minus_elsewhere", [NS, NS])
        zn, en = sb("new_logits", [NS, 8, NS]), sb("new_exp", [NS, 8, NS])
        en2, wn2 = sb("new_softplus_by_seq", [NS, NSEQ, 64]), sb("new_weights_by_seq", [NS, NSEQ, 64])
        wns = sb("new_weights_of_seq", [NS, 2, 64])
        vn = sb("v_new", [NS, 512])
        own = sb("own_head_blocks", [NS, 512])
        sel = sb("query_selector", [NS, 8])
        om = zn[:, :, :].rearrange("p h c -> p (h c)")
        (tab_in, k_in0, k_in1, v_in0, v_in1, vn_in, masks, prep, new_qk, new_s, new_act) = (sem(n) for n in (
            "table_in", "k_in_even", "k_in_odd", "v_in_even", "v_in_odd", "vn_in", "masks", "prep", "new_qk", "new_s",
            "new_act"))
        new_z = sem("new_z")
        (tr_done, a_copied, d_copied, qk_done, z_read, e_ready, ln_ready, sp_ready, suf_ready, s_done, d_ready,
         w_ready, pv_done, om_ready, fin_done, f_read, act_step, pool_step) = (sem(n) for n in (
             "tr_done", "a_copied", "d_copied", "qk_done", "z_read", "e_ready", "ln_ready", "sp_ready", "suf_ready",
             "s_done", "d_ready", "w_ready", "pv_done", "om_ready", "fin_done", "f_read", "act_step", "pool_step"))
        block = ctx.enter_context(nc.Block())
        k_in, v_in = (k_in0, k_in1), (v_in0, v_in1)

        def steps(eng, step, order=None, per=0):
            step(0, 0, 0)
            with eng.Fori(0, 3) as i:
                if order:
                    order.enter(i, 2 * per)
                step(2 * i + 1, 1, i)
                step(2 * i + 2, 0, i + 1)
                if order:
                    order.leave(3)
            step(NSEQ - 1, 1, 3)

        @block.sync
        def _(sp):
            sp.dma_start(table[:, :], dr["page_table"].rearrange("(o s) p -> o (s p)", o=1)).then_inc(tab_in, 16)
            sp.dma_start(vn[:, :], dr["v_sample"][0].rearrange("s t h d -> (s t) (h d)")).then_inc(vn_in, 16)
            sp.wait_ge(tab_in, 16)
            k_dram = dr["cache_k"][0].rearrange("n t h d -> n t (h d)")
            v_dram = dr["cache_v"][0].rearrange("n t h d -> n t (h d)")
            n_pool = k_dram.shape[0]
            with sp.Fori(0, 4) as i:
                for slot in range(2):
                    s = 2 * i + slot
                    for pages, cache, arrived, free, value in ((kp, k_dram, k_in, tr_done, 8 * s + 8),
                                                               (vp, v_dram, v_in, pv_done, s + 1)):
                        for pg in range(PAGES):
                            number = sp.value_load(
                                table[:, bass.ds(s * PAGES + pg, 1)].bitcast(mybir.dt.int32)[0:1, 0:1],
                                min_val=0, max_val=n_pool - 1)
                            if pg == 0:
                                sp.wait_ge(free, value)
                            sp.dma_start(pages[:, slot, pg, :],
                                         cache[bass.ds(number, 1)].rearrange("o t c -> (o t) c")
                                         ).then_inc(arrived[slot], 16)

        @block.gpsimd
        def _(pool):
            def select(out, in_, pattern, base, mult, op, n, fill=0.0):
                pool.affine_select(out=out, in_=in_, compare_op=op, fill=fill, base=base, pattern=pattern,
                                   channel_multiplier=mult).then_inc(masks, 1)
                pool.wait_ge(masks, n)

            grid = "p (a b) -> p a b"
            pool.memset(gone[:, :], 0.0).then_inc(masks, 1)
            pool.wait_ge(masks, 1)
            select(same[:, :], core.ones[0:NS, 0:NS], [[1, NS]], 0, -1, ALU.is_gt, 2)
            sv, gv = same[:, :].rearrange(grid, b=8), gone[:, :].rearrange(grid, b=8)
            select(sv, sv, [[-8, 8], [0, 8]], 0, 1, ALU.is_ge, 3)
            select(gone[:, :], gone[:, :], [[1, NS]], 0, -1, ALU.is_gt, 4, MASKED)
            select(gv, gv, [[-8, 8], [0, 8]], 0, 1, ALU.is_ge, 5, MASKED)
            pool.memset(own[:, :], 1.0).then_inc(masks, 1)
            pool.wait_ge(masks, 6)
            ov = own[:, :].rearrange(grid, b=HD)
            select(ov, ov, [[-8, 8], [0, HD]], 0, 1, ALU.is_ge, 7)
            select(ov, ov, [[8, 8], [0, HD]], 7, -1, ALU.is_ge, 8)
            pool.memset(sel[:, :], 0.0).then_inc(masks, 1)
            pool.wait_ge(masks, 9)
            for h in range(8):
                select(sel[:, :], sel[:, :], [[-1, 8]], -8 * h, 1, ALU.not_equal, 10 + h, 1.0)
            o = Order(pool, pool_step)

            def step(s, slot, half):
                e = es[:, slot, :, :]
                pool.wait_ge(s_done, s + 1)
                pool.wait_ge(sp_ready, s + 1)
                o.did(pool.tensor_tensor(suf[:, 6, :], e[:, 7, :], core.ones[:, 0:64], ALU.mult))
                for pg in range(5, -1, -1):
                    o.after()
                    ins = pool.tensor_tensor(suf[:, pg, :], suf[:, pg + 1, :], e[:, pg + 1, :], ALU.add)
                    if pg:
                        o.did(ins)
                    else:
                        o.raises(ins, suf_ready, 2 * s + 1)
                pool.wait_ge(pv_done, s + 1)
                pool.tensor_tensor(wns[:, slot, :], wn2[:, bass.ds(s, 1), :].rearrange("p o c -> p (o c)"),
                                   core.ones[0:NS, 0:64], ALU.mult).then_inc(suf_ready, 1)

            pool.wait_ge(new_act, 4)
            steps(pool, step, o, 6)

        @block.tensor
        def _(pe):
            pe.sem_inc(tr_done, 16)
            pe.sem_inc(qk_done, 1)
            pe.sem_inc(s_done, 1)
            pe.sem_inc(pv_done, 2)
            pe.wait_ge(prep, 3)
            for h in range(8):
                mm = pe.matmul(core.ps[0:NS, 5, h * NS:(h + 1) * NS], k_sample[:, h // 2, :],
                               qd[:, h // 2, :, 8 * (h % 2):8 * (h % 2) + 8], start=True, stop=True)
            mm.then_inc(new_qk, 1)
            pe.wait_ge(vn_in, 16)
            pe.wait_ge(prep, 6)
            pe.matmul(core.ps[0:NS, 6, :], core.tri[0:NS, 0:NS], en[:, :, :].rearrange("p h c -> p (h c)"),
                      start=True, stop=True).then_inc(new_s, 1)
            pe.wait_ge(prep, 8)
            pe.wait_ge(masks, 17)

            def values(s, slot, half):
                pe.wait_ge(w_ready, s + 1)
                pe.wait_ge(suf_ready, 2 * s + 2)
                pe.wait_ge(v_in[slot], 128 * half + 128)
                pe.wait_ge(om_ready, s + 1)
                for pg in range(PAGES):
                    pe.matmul(core.ps[0:64, 6, :], zs[:, slot, pg, :], vp[:, slot, pg, :],
                              start=pg == 0, stop=False)
                pe.matmul(core.ps[0:64, 6, :], wns[:, slot, :], vn[:, :], start=False, stop=True
                          ).then_inc(pv_done, 1)

            def finish(s):
                pe.wait_ge(f_read, s + 1)
                pe.wait_ge(om_ready, s + 2)
                for c in range(4):
                    mm = pe.matmul(core.ps[:, 7, 8 * c:8 * c + 8], om[:, c * P:(c + 1) * P], sel[:, :],
                                   start=True, stop=True)
                mm.then_inc(fin_done, 1)

            def step(s, slot, half, back=None):
                pe.wait_ge(k_in[slot], 128 * half + 128)
                for g in range(8):
                    c, h4 = g // 2, g % 2
                    pe.wait_ge(a_copied if g % 2 == 0 else d_copied, 4 * s + g // 2 + 1)
                    for q in range(4):
                        mm = pe.transpose(core.ps[:, g % 4, q * P:(q + 1) * P],
                                          kp[:, slot, 4 * h4 + q, c * P:(c + 1) * P], core.ident[:, :])
                    mm.then_inc(tr_done, 1)
                pe.wait_ge(z_read, s + 1)
                pe.wait_ge(a_copied, 4 * s + 6)
                pe.wait_ge(d_copied, 4 * s + 6)
                for pg in range(PAGES):
                    for c in range(4):
                        mm = pe.matmul(core.ps[:, 4, pg * 64 + c * 16:pg * 64 + c * 16 + 16],
                                       ktr[:, c, pg * P:(pg + 1) * P],
                                       qd[:, c, bass.ds(s, 1), :].rearrange("p o n -> p (o n)"),
                                       start=True, stop=True)
                mm.then_inc(qk_done, 1)
                if back:
                    values(*back)
                pe.wait_ge(d_ready, s + 1)
                pe.wait_ge(sp_ready, s + 1)
                e = es[:, slot, :, :].rearrange("p a b -> p (a b)")
                pe.matmul(core.ps[:, 5, :], core.tri[:, :], e, start=True, stop=False)
                pe.matmul(core.ps[:, 5, :].rearrange("p (a b) -> p a b", a=8), core.ones[0:NS, :],
                          en2[:, bass.ds(s, 1), :].to_broadcast((NS, 8, 64)), start=False, stop=False)
                pe.wait_ge(suf_ready, 2 * s + 1)
                pe.matmul(core.ps[:, 5, 0:448], core.ones[:, :], suf[:, :, :].rearrange("p a b -> p (a b)"),
                          start=False, stop=True).then_inc(s_done, 1)
                if back:
                    finish(back[0])

            step(0, 0, 0)
            with pe.Fori(0, 3) as i:
                step(2 * i + 1, 1, i, (2 * i, 0, i))
                step(2 * i + 2, 0, i + 1, (2 * i + 1, 1, i))
            step(7, 1, 3, (6, 0, 3))
            values(7, 1, 3)
            finish(7)

        @block.scalar
        def _(act):
            act.sem_inc(a_copied, 2)
            flat = "p h c -> p (h c)"
            act.preload_act_table_set("natural_log_exp_and_others")
            act.wait_ge(prep, 5)
            act.activation(en[:, :, :].rearrange(flat), en[:, :, :].rearrange(flat), ACT.Exp).then_inc(new_act, 1)
            act.wait_ge(new_act, 1)
            act.activation(en[:, :, :].rearrange(flat), en[:, :, :].rearrange(flat), ACT.Ln, bias=1.0
                           ).then_inc(new_act, 1)
            act.wait_ge(prep, 9)
            act.activation(wn2[:, :, :].rearrange(flat), wn2[:, :, :].rearrange(flat), ACT.Exp).then_inc(new_act, 1)
            act.wait_ge(new_act, 3)
            act.sem_inc(new_act, 1)
            o = Order(act, act_step)

            def step(s, slot, half):
                act.wait_ge(qk_done, s + 1)
                for g in range(0, 8, 2):
                    act.wait_ge(tr_done, 8 * s + g + 17)
                    act.copy(ktr[:, g // 2, 0:512], core.ps[:, g % 4, :]).then_inc(a_copied, 1)
                e = es[:, slot, :, :].rearrange("p a b -> p (a b)")
                z = zs[:, slot, :, :].rearrange("p a b -> p (a b)")
                act.wait_ge(e_ready, s + 1)
                o.did(act.activation(e, e, ACT.Exp))
                o.after()
                act.activation(e, e, ACT.Ln, bias=1.0).then_inc(ln_ready, 1)
                act.wait_ge(d_ready, s + 2)
                act.activation(z, z, ACT.Exp).then_inc(w_ready, 1)

            steps(act, step, o, 1)

        @block.vector
        def _(dve):
            def did(ins, n):
                ins.then_inc(prep, 1)
                dve.wait_ge(prep, n)

            for credit, v in ((d_copied, 2), (z_read, 1), (d_ready, 1), (om_ready, 1), (f_read, 1)):
                dve.sem_inc(credit, v)
            did(dve.memset(qd[:, :, :, :], 0.0), 1)
            for h in range(2):
                b = h * HD
                did(dve.tensor_copy(qd[b:b + HD, :, :, 8 * h:8 * h + 8],
                                    mix[b:b + HD, 0:4, SEQ:SEQ + NS].rearrange("p c (s q) -> p c s q", q=SLEN)),
                    2 + h)
            dve.wait_ge(new_qk, 1)
            dve.tensor_copy(brow[:, :, :], core.bias[:, :].unsqueeze(2).to_broadcast((P, 8, 8))).then_inc(prep, 1)
            dve.wait_ge(prep, 4)
            dve.scalar_tensor_tensor(zn[:, :, :], core.ps[0:NS, 5, :].rearrange("p (h c) -> p h c", h=8), 0.125,
                                     core.bias[0:NS, :].unsqueeze(2).to_broadcast((NS, 8, NS)),
                                     ALU.mult, ALU.add).then_inc(new_z, 1)
            dve.wait_ge(new_z, 1)
            did(dve.tensor_scalar(en[:, :, :], zn[:, :, :], ZCAP, None, ALU.min), 5)
            dve.wait_ge(new_act, 2)
            dve.tensor_tensor(en[:, :, :], zn[:, :, :], en[:, :, :], ALU.max).then_inc(new_z, 1)
            dve.wait_ge(new_z, 2)
            dve.wait_ge(masks, 5)
            did(dve.tensor_tensor(en[:, :, :], en[:, :, :], same[:, :].unsqueeze(1).to_broadcast((NS, 8, NS)),
                                  ALU.mult), 6)
            by_seq = "p h (s q) -> p s h q"
            did(dve.tensor_copy(en2[:, :, :].rearrange("p s (h q) -> p s h q", q=8),
                                en[:, :, :].rearrange(by_seq, q=8)), 7)
            dve.wait_ge(new_s, 1)
            did(dve.tensor_tensor(zn[:, :, :], zn[:, :, :], core.ps[0:NS, 6, :].rearrange("p (h c) -> p h c", h=8),
                                  ALU.subtract), 8)
            dve.tensor_tensor(wn2[:, :, :].rearrange("p s (h q) -> p s h q", q=8),
                              zn[:, :, :].rearrange(by_seq, q=8),
                              gone[:, :].rearrange("p (s q) -> p s q", q=8).unsqueeze(2).to_broadcast((NS, 8, 8, 8)),
                              ALU.add).then_inc(prep, 1)

            def masked(s):
                dve.wait_ge(f_read, s + 1)
                dve.wait_ge(pv_done, s + 3)
                dve.tensor_tensor(om[:, :], core.ps[0:64, 6, :], own[:, :], ALU.mult).then_inc(om_ready, 1)

            def store(s):
                dve.wait_ge(fin_done, s + 1)
                dve.tensor_scalar(mix[:, 0:4, bass.ds(8 * s + SEQ, 8)],
                                  core.ps[:, 7, 0:32].rearrange("p (c q) -> p c q", q=8), 1.0, None, ALU.mult
                                  ).then_inc(f_read, 1)

            def step(s, slot, half, back=None):
                dve.wait_ge(qk_done, s + 1)
                for g in range(1, 8, 2):
                    dve.wait_ge(tr_done, 8 * s + g + 17)
                    dve.tensor_copy(ktr[:, g // 2, 512:1024], core.ps[:, g % 4, :]).then_inc(d_copied, 1)
                dve.wait_ge(qk_done, s + 2)
                z, e = zs[:, slot, :, :], es[:, slot, :, :]
                dve.scalar_tensor_tensor(z, core.ps[:, 4, :].rearrange("p (a b) -> p a b", a=8), 0.125,
                                         brow[:, :, :].rearrange("p h q -> p (h q)").unsqueeze(1)
                                         .to_broadcast((P, 8, 64)), ALU.mult, ALU.add).then_inc(z_read, 1)
                dve.wait_ge(z_read, s + 2)
                dve.tensor_scalar(e, z, ZCAP, None, ALU.min).then_inc(e_ready, 1)
                dve.wait_ge(ln_ready, s + 1)
                dve.tensor_tensor(e, z, e, ALU.max).then_inc(sp_ready, 1)
                if back is not None:
                    masked(back)
                dve.wait_ge(s_done, s + 2)
                dve.tensor_tensor(z, z, core.ps[:, 5, :].rearrange("p (a b) -> p a b", a=8), ALU.subtract
                                  ).then_inc(d_ready, 1)
                if back is not None:
                    store(back)

            step(0, 0, 0)
            with dve.Fori(0, 3) as i:
                step(2 * i + 1, 1, i, 2 * i)
                step(2 * i + 2, 0, i + 1, 2 * i + 1)
            step(7, 1, 3, 6)
            masked(7)
            store(7)


def phase_out(core, act_hi, act_lo, src, weight, tag, next_slabs):
    core.phase = ""
    nc, w = core.nc, core.w
    n0 = core.slabs
    with ExitStack() as ctx:
        def sem(name):
            return core.sem(name + tag)

        hi_ready, lo_ready, evac = sem("src_hi"), sem("src_lo"), sem("evac")
        block = ctx.enter_context(nc.Block())

        @block.sync
        def _(sp):
            with sp.Fori(0, 3) as i:
                for par in range(2):
                    w.load(sp, n0 + 2 * i + 2 + par, par, square_slab(weight, (2 * i + 2 + par) * P))
            for par in range(2):
                w.load(sp, n0 + 8 + par, par, next_slabs[par])

        @block.gpsimd
        def _(pool):
            with pool.Fori(0, 4) as i:
                for par in range(2):
                    w.split_lo(pool, n0 + 2 * i + 2 + par, par)

        @block.tensor
        def _(pe):
            def job(i, par, x_ready=None):
                w.wait_ready(pe, n0 + 2 * i + par)
                pe.wait_ge(evac, 2 * i + par + 1)
                dense(pe, (core.bank_a, core.bank_b)[par],
                      [(w.hi[:, par, k * P:(k + 1) * P], w.lo[:, par, k * P:(k + 1) * P],
                        act_hi[:, k, :], act_lo[:, k, :]) for k in range(KT)], x_ready).then_inc(w.used, 1)

            job(0, 0, lambda k: pe.wait_ge(lo_ready, k + 1))
            job(0, 1)
            with pe.Fori(1, 4) as i:
                job(i, 0)
                job(i, 1)

        @block.scalar
        def _(act):
            for k in range(KT):
                act.activation(act_hi[:, k, :], src[:, k, :], ACT.Copy).then_inc(hi_ready, 1)
            with act.Fori(0, 4) as i:
                for par in range(2):
                    w.split_hi(act, n0 + 2 * i + 2 + par, n0 // 2 + i + 1, par)

        @block.vector
        def _(dve):
            dve.sem_inc(evac, 2)
            for k in range(KT):
                dve.wait_ge(hi_ready, k + 1)
                dve.tensor_tensor(act_lo[:, k, :], src[:, k, :], act_hi[:, k, :].bitcast(F32), ALU.subtract
                                  ).then_inc(lo_ready, 1)
            with dve.Fori(0, 4) as i:
                for par in range(2):
                    w.wait_job(dve, n0 + 2 * i + par)
                    tile = core.x[:, bass.ds(2 * i + par, 1), :].rearrange("p o (c n) -> p (o c) n", c=3)
                    dve.tensor_tensor(tile, tile, (core.bank_a, core.bank_b)[par][:, :, 0:CH], ALU.add
                                      ).then_inc(evac, 1)
    core.slabs += 8



def phase_ffn(core, layer, act_hi, act_lo, next_slabs):
    core.phase = ""
    nc, dr, w = core.nc, core.dram, core.w
    n0, j0 = core.slabs, core.slabs - w.skew
    TURNS = FT // 2
    tag = f"_ffn{layer}"
    w_gate, w_up, w_down = dr["w_gate"][layer], dr["w_up"][layer], dr["w_down"][layer]
    with ExitStack() as ctx:
        def sb(name, shape, dt=F32):
            return ctx.enter_context(nc.sbuf_tensor(name + tag, shape, dt))

        def sem(name):
            return core.sem(name + tag)

        h_hi, h_lo = sb("hidden_hi", [P, 2, T], F32R), sb("hidden_lo", [P, 2, T], F32R)
        d_hi, d_lo = sb("w_down_hi", [P, 2, D], F32R), sb("w_down_lo", [P, 2, D], F32R)
        gb = sb("gate_padded", [P, T + 4])
        gc, hb = sb("gate_conv", [P, T]), sb("hidden", [P, T])
        xs = sb("gate_sample", [P, NSEQ, 2 + SLEN])
        rows = sb("state_rows", [18, FF])
        prow, par = sb("param_rows", [96, P]), sb("params", [P, 96])
        state = sb("state_columns", [P, FT, 16])
        pk = sb("new_state_columns", [P, FT, 18])
        norm = Norm(core, ctx, tag, act_hi, act_lo, gc, [hb[:, :], gb[:, 2:2 + T]], lambda k: core.g_ffn(layer, k))
        (small_in, small_tr, small_copied, evac, gc_ready, gelu_ready, gr_ready, hh_ready, hl_ready, down_done,
         rows_tr, rows_copied, stored, dve_step) = (sem(n) for n in (
             "small_in", "small_tr", "small_copied", "evac", "gc_ready", "gelu_ready", "gr_ready", "hh_ready",
             "hl_ready", "down_done", "rows_tr", "rows_copied", "stored", "dve_step"))
        block = ctx.enter_context(nc.Block())

        def turns(eng, body, order=None, per=0):
            with eng.Fori(0, TURNS - 1) as i:
                if order:
                    order.enter(i, per)
                body(i, False)
                if order:
                    order.leave(TURNS - 1)
            body(TURNS - 1, True)

        @block.sync
        def _(sp):
            sp.dma_start(rows[0:16, :], dr["state_ffn_conv"][layer].rearrange("s j c -> (s j) c")).then_inc(small_in, 16)
            sp.dma_start(prow[0:72, :], dr["w_ffn_conv"][layer].rearrange("j (r c) -> (j r) c", c=P)).then_inc(small_in, 16)
            sp.dma_start(prow[72:96, :], dr["b_ffn_conv"][layer].rearrange("(r c) -> r c", c=P)).then_inc(small_in, 16)
            w.load(sp, n0 + 2, 0, square_slab(w_gate, P))

            def body(i, last):
                n = n0 + 6 * i
                w.load(sp, n + 3, 1, square_slab(w_up, (2 * i + 1) * P))
                if last:
                    w.load(sp, n + 4, 0, w_down[2 * i * P:(2 * i + 1) * P, :])
                    w.load(sp, n + 5, 1, w_down[(2 * i + 1) * P:(2 * i + 2) * P, :])
                    for par_, src in enumerate(next_slabs):
                        w.load(sp, n + 6 + par_, par_, src)
                    return
                w.load(sp, n + 4, 0, square_slab(w_gate, (2 * i + 2) * P))
                w.load(sp, n + 5, 1, w_down[bass.ds(2 * i * P, P), :])
                w.load(sp, n + 6, 0, w_down[bass.ds((2 * i + 1) * P, P), :])
                w.load(sp, n + 7, 1, square_slab(w_up, (2 * i + 2) * P))
                w.load(sp, n + 8, 0, square_slab(w_gate, (2 * i + 3) * P))

            turns(sp, body)
            sp.wait_ge(rows_copied, 6)
            sp.dma_start(dr["ffn_conv_prompt"][layer, 0], rows[0:2, :]).then_inc(stored, 16)
            sp.dma_start(dr["ffn_conv_sample"][layer].rearrange("s j c -> (s j) c"), rows[2:18, :]).then_inc(stored, 16)
            sp.wait_ge(stored, 32)

        @block.gpsimd
        def _(pool):
            def gate_scale(f):
                pool.wait_ge(gelu_ready, f + 1)
                pool.tensor_tensor(gc[:, :], gc[:, :], core.rb[:, :], ALU.mult).then_inc(gr_ready, 1)

            def gu(n, slot):
                w.split_lo_at(pool, n, slot, w.hi[:, slot, :], w.lo[:, slot, :])

            def down(n, raw, k):
                w.split_lo_at(pool, n, raw, d_hi[:, k, :], d_lo[:, k, :])

            gu(n0 + 2, 0)
            gate_scale(0)

            def body(i, last):
                n = n0 + 6 * i
                gu(n + 3, 1)
                if last:
                    gate_scale(2 * i + 1)
                    down(n + 4, 0, 0)
                    down(n + 5, 1, 1)
                    for k in range(len(next_slabs)):
                        gu(n + 6 + k, k)
                    return
                gu(n + 4, 0)
                gate_scale(2 * i + 1)
                down(n + 5, 1, 0)
                down(n + 6, 0, 1)
                gu(n + 7, 1)
                gate_scale(2 * i + 2)
                gu(n + 8, 0)

            turns(pool, body)

        @block.tensor
        def _(pe):
            pe.sem_inc(down_done, 8)

            def gu(n, q, slot, x_ready=None):
                w.wait_ready(pe, n)
                pe.wait_ge(evac, q + 1)
                dense(pe, (core.bank_a, core.bank_b)[slot],
                      [(w.hi[:, slot, k * P:(k + 1) * P], w.lo[:, slot, k * P:(k + 1) * P],
                        act_hi[:, k, :], act_lo[:, k, :]) for k in range(KT)], x_ready).then_inc(w.used, 1)

            def state_columns(k):
                pe.wait_ge(norm.s_lo, k + 1)
                if k != 2:
                    return
                pe.wait_ge(small_in, 48)
                for f in range(FT):
                    pe.transpose(core.ps[:, 6, 16 * f:16 * f + 16], rows[0:16, f * P:(f + 1) * P],
                                 core.ident[0:16, 0:16])
                pe.transpose(core.ps[:, 7, 0:96], prow[:, :], core.ident[0:96, 0:96]).then_inc(small_tr, 1)

            gu(n0, 0, 0, state_columns)
            pe.wait_ge(small_copied, 2)
            norm.sums_pe(pe)

            def body(i, last):
                n, q = n0 + 6 * i, 12 * i
                gu(n + 1, q + 1, 1)
                gu(n + 2, q + 2, 0)
                gu(n + 3, q + 3, 1)
                if not last:
                    gu(n + 4, q + 4, 0)
                w.wait_ready(pe, n + 6 - last)
                pe.wait_ge(hl_ready, 2 * i + 2)
                for m in range(KT):
                    c = slice(m * P, (m + 1) * P)
                    pe.wait_ge(evac, q + 6 - last + m)
                    dense(pe, (core.bank_a, core.bank_b)[(m + 1 - last) % 2],
                          [(d_hi[:, k, c], d_lo[:, k, c], h_hi[:, k, :], h_lo[:, k, :]) for k in range(2)]
                          ).then_inc(down_done, 1)

            turns(pe, body)
            pe.wait_ge(evac, 12 * TURNS + 2)
            for f in range(FT):
                mm = pe.transpose(core.ps[0:18, f // 4, (f % 4) * P:(f % 4 + 1) * P], pk[:, f, :], core.ident[:, :])
            mm.then_inc(rows_tr, 1)

        @block.scalar
        def _(act):
            def split(what, n, half, slot, raw, j=None):
                if what == "gu":
                    w.split_hi_at(act, n, half, raw, w.hi[:, slot, :], (w.used, j + 1))
                else:
                    w.split_hi_at(act, n, half, raw, d_hi[:, int(what[1]), :], j)

            norm.split_act(act)
            act.wait_ge(small_tr, 1)
            act.copy(state[:, :, :], core.ps[:, 6, 0:384].rearrange("p (f c) -> p f c", c=16)).then_inc(small_copied, 1)
            act.copy(par[:, :], core.ps[:, 7, 0:96]).then_inc(small_copied, 1)
            norm.squares_act(act)
            norm.roots_act(act)
            split("gu", n0 + 2, n0 // 2 + 1, 0, 0, j0 + 2)

            def gelu(f):
                act.wait_ge(gc_ready, f + 1)
                act.activation(gc[:, :], gc[:, :], ACT.Gelu_apprx_tanh).then_inc(gelu_ready, 1)

            def hidden_hi(i, k):
                act.wait_ge(down_done, 8 * i + 8)
                act.wait_ge(evac, 12 * i + 2 * k + 4)
                act.activation(h_hi[:, k, :], hb[:, :], ACT.Copy).then_inc(hh_ready, 1)

            gelu(0)

            def body(i, last):
                n, j, half = n0 + 6 * i, j0 + 4 * i, n0 // 2 + 3 * i
                used_up = (down_done, 8 * i + 8)
                split("gu", n + 3, half + 1, 1, 1, j + 3)
                hidden_hi(i, 0)
                if last:
                    gelu(2 * i + 1)
                    split("d0", n + 4, half + 2, None, 0, used_up)
                    split("d1", n + 5, half + 2, None, 1, used_up)
                    hidden_hi(i, 1)
                    for k in range(len(next_slabs)):
                        split("gu", n + 6 + k, half + 3, k, k, j + 4 + k)
                    return
                split("gu", n + 4, half + 2, 0, 0, j + 4)
                gelu(2 * i + 1)
                split("d0", n + 5, half + 2, None, 1, used_up)
                split("d1", n + 6, half + 3, None, 0, used_up)
                hidden_hi(i, 1)
                split("gu", n + 7, half + 3, 1, 1, j + 5)
                gelu(2 * i + 2)
                split("gu", n + 8, half + 4, 0, 0, j + 6)

            turns(act, body)
            act.wait_ge(rows_tr, 1)
            for b in range(3):
                act.copy(rows[:, b * 512:(b + 1) * 512], core.ps[0:18, b, :]).then_inc(rows_copied, 1)

        @block.vector
        def _(dve):
            o = Order(dve, dve_step)
            dve.sem_inc(evac, 2)
            norm.split_dve(dve)
            norm.sums_dve(dve)
            o.did(dve.memset(gb[:, 0:2], 0.0))
            o.after()
            norm.scale_dve(dve)
            dve.wait_ge(small_copied, 2)

            def gate(i, r, q, slot, between=None):
                f = 2 * i + r
                w.wait_job(dve, job_slab(i, r))
                dve.tensor_tensor(chunks(gb[:, 2:2 + T]), (core.bank_a, core.bank_b)[slot][:, :, 0:CH],
                                  chunks(core.rb[:, :]), ALU.mult).then_inc(evac, 1)

                def tap(j):
                    return par[:, bass.ds(f + FT * j, 1)]

                dve.wait_ge(evac, q + 3)
                o.did(dve.tensor_scalar(gc[:, :], gb[:, 2:2 + T], tap(2), tap(3), ALU.mult, ALU.add))
                o.did(dve.tensor_copy(xs[:, :, 0:2], state[:, bass.ds(f, 1), :]
                                      .rearrange("p o (s j) -> p (o s) j", j=2)))
                o.did(dve.tensor_copy(xs[:, :, 2:2 + SLEN],
                                      gb[:, 2 + SEQ:2 + SEQ + NS].rearrange("p (s t) -> p s t", t=SLEN)))
                for j in (1, 0):
                    if between:
                        between(1 - j)
                    o.after()
                    o.did(dve.scalar_tensor_tensor(gc[:, :], gb[:, j:j + T], tap(j), gc[:, :], ALU.mult, ALU.add))
                gcs = gc[:, SEQ:SEQ + NS].rearrange("p (s t) -> p s t", t=SLEN)
                o.after()
                o.did(dve.tensor_scalar(gcs, xs[:, :, 2:2 + SLEN], tap(2), tap(3), ALU.mult, ALU.add))
                o.did(dve.tensor_copy(pk[:, bass.ds(f, 1), 0:2], gb[:, SEQ:SEQ + 2]))
                o.did(dve.tensor_copy(pk[:, bass.ds(f, 1), 2:18].rearrange("p o (s j) -> p (o s) j", j=2),
                                      xs[:, :, SLEN:2 + SLEN]))
                o.after()
                o.did(dve.scalar_tensor_tensor(gcs, xs[:, :, 1:1 + SLEN], tap(1), gcs, ALU.mult, ALU.add))
                o.after()
                dve.scalar_tensor_tensor(gcs, xs[:, :, 0:SLEN], tap(0), gcs, ALU.mult, ALU.add).then_inc(gc_ready, 1)

            def job_slab(i, r):
                return n0 + 4 * i + 2 * r

            def up(i, k):
                w.wait_job(dve, n0 + 4 * i + 1 + 2 * k)
                dve.wait_ge(gr_ready, 2 * i + k + 1)
                dve.tensor_tensor(chunks(hb[:, :]), core.bank_b[:, :, 0:CH], chunks(gc[:, :]), ALU.mult
                                  ).then_inc(evac, 1)
                dve.wait_ge(hh_ready, 2 * i + k + 1)
                dve.tensor_tensor(h_lo[:, k, :], hb[:, :], h_hi[:, k, :].bitcast(F32), ALU.subtract
                                  ).then_inc(hl_ready, 1)

            gate(0, 0, 0, 0)

            def body(i, last):
                q = 12 * i
                dve.wait_ge(gc_ready, 2 * i + 1)
                up(i, 0)
                gate(i, 1, q + 2, 0)
                up(i, 1)

                def residual(m):
                    dve.wait_ge(down_done, 8 * i + 9 + m)
                    dve.tensor_tensor(chunks(core.x[:, m, :]), chunks(core.x[:, m, :]),
                                      (core.bank_a, core.bank_b)[(m + 1 - last) % 2][:, :, 0:CH], ALU.add
                                      ).then_inc(evac, 1)

                if not last:
                    gate(i, 2, q + 4, 0, residual)
                for m in range(0 if last else 2, KT):
                    residual(m)

            turns(dve, body, o, 18)
            dve.wait_ge(rows_tr, 1)
            for b in range(3, 6):
                dve.tensor_copy(rows[:, b * 512:(b + 1) * 512], core.ps[0:18, b, :]).then_inc(rows_copied, 1)
    core.slabs += 3 * FT
    w.skew += FT


def phase_odd(core, act_hi, act_lo, uv, next_slabs):
    core.phase = ""
    nc, dr, w = core.nc, core.dram, core.w
    n0 = core.slabs
    with ExitStack() as ctx:
        def sb(name, shape, dt=F32):
            return ctx.enter_context(nc.sbuf_tensor(name + "_odd", shape, dt))

        def sem(name):
            return core.sem(name + "_odd")

        vb, sq, rv, ub = (sb(n, [P, T]) for n in ("v_head", "v_squares", "v_scale", "u_head"))
        vtok = sb("v_tokens", [P, 9, P])
        wt, wb = sb("mix_weights", [P, 8, P]), sb("mix_weights_sample", [NS, 8, NS])
        bs = sb("mix_bias", [P, 8, P])
        wraw = ub[:, 0:1024].rearrange("p (h s) -> p h s", h=8)
        braw = rv[0:NS, 0:512].rearrange("p (h s) -> p h s", h=8)
        norm = Norm(core, ctx, "_odd", act_hi, act_lo, vb, [uv[:, 0, :], uv[:, 1, :]], lambda k: core.g_mix(1, k))
        (w_in, b_zero, prep_tr, prep_copied, masked, evac, v_gelu, sq_ready, v_sum_mm, root_read, vn_ready, u_gelu,
         v_tr, tok_ready, tok_free, tok_out, mix_mm, mix_read, dve_step, act_step) = (sem(n) for n in (
             "spatial_in", "b_zero", "prep_tr", "prep_copied", "masked", "evac", "v_gelu", "sq_ready", "v_sum_mm",
             "root_read", "vn_ready", "u_gelu", "v_tr", "tok_ready", "tok_free", "tok_out", "mix_mm", "mix_read",
             "dve_step", "act_step"))
        tok_copied, root_ready = sem("tok_copied"), sem("root_ready")
        block = ctx.enter_context(nc.Block())
        w_odd = dr["w_in_odd"][0]

        @block.sync
        def _(sp):
            sp.dma_start(wraw, dr["w_spatial"][0].rearrange("h t s -> t h s")).then_inc(w_in, 16)
            sp.dma_start(bs[:, :, :].rearrange("p h t -> p (h t)"), dr["b_spatial"].rearrange("o h t -> o (h t)")
                         .to_broadcast((P, 8 * P))).then_inc(w_in, 16)
            sp.wait_ge(b_zero, 1)
            for s in range(NSEQ):
                sp.dma_start(braw[8 * s:8 * s + 8, :, 8 * s:8 * s + 8],
                             dr["w_spatial"][0, :, 0:SLEN, 0:SLEN].rearrange("h t s -> t h s")).then_inc(w_in, 16)

            def rows_out(h):
                sp.wait_ge(tok_ready, h + 1)
                c = bass.ds(h * P, P)
                sp.dma_start(dr["chunk_v_prompt"][0, 0, :, c], vtok[:, 7, :]).then_inc(tok_out, 16)
                sp.dma_start(dr["chunk_v_sample"][0].rearrange("s t c -> (s t) c")[:, c], vtok[0:NS, 8, :]
                             ).then_inc(tok_out, 16)
                sp.wait_ge(tok_out, 32 * h + 32)
                sp.sem_inc(tok_free, 1)

            sp.sem_inc(tok_free, 1)
            with sp.Fori(0, 7) as h:
                w.load(sp, n0 + 2 * h + 2, 0, square_slab(w_odd, (h + KT + 1) * P))
                w.load(sp, n0 + 2 * h + 3, 1, square_slab(w_odd, (h + 1) * P))
                rows_out(h)
            for par in range(2):
                w.load(sp, n0 + 16 + par, par, next_slabs[par])
            rows_out(7)

        @block.gpsimd
        def _(pool):
            pool.memset(braw, 0.0).then_inc(b_zero, 1)
            pool.wait_ge(prep_copied, 3)
            for m, n in ((wt, P), (wb, NS)):
                pool.affine_select(out=m[:, :, :], in_=m[:, :, :], compare_op=ALU.is_ge, fill=0.0, base=0,
                                   pattern=[[0, 8], [1, n]], channel_multiplier=-1).then_inc(masked, 1)
            with pool.Fori(0, 8) as h:
                for par in range(2):
                    w.split_lo(pool, n0 + 2 * h + 2 + par, par)

        @block.tensor
        def _(pe):
            def job(n, slot, x_ready=None):
                w.wait_ready(pe, n0 + n)
                pe.wait_ge(evac, n + 1)
                dense(pe, (core.bank_a, core.bank_b)[slot],
                      [(w.hi[:, slot, k * P:(k + 1) * P], w.lo[:, slot, k * P:(k + 1) * P],
                        act_hi[:, k, :], act_lo[:, k, :]) for k in range(KT)], x_ready).then_inc(w.used, 1)

            job(0, 0, lambda k: pe.wait_ge(norm.s_lo, k + 1))
            pe.wait_ge(w_in, 160)
            for h in range(8):
                pe.transpose(core.ps[:, 3 + h // 4, (h % 4) * P:(h % 4 + 1) * P], wraw[:, h, :], core.ident[:, :])
                mm = pe.transpose(core.ps[0:NS, 5, h * NS:(h + 1) * NS], braw[:, h, :], core.ident[0:NS, 0:NS])
            mm.then_inc(prep_tr, 1)
            norm.sums_pe(pe)
            pe.wait_ge(prep_copied, 3)

            def turn(h, last):
                pe.wait_ge(mix_read, 3 * h + 1)
                job(2 * h + 1, 1)
                pe.wait_ge(mix_read, 3 * h + 3)
                pe.wait_ge(sq_ready, h + 1)
                for c in range(3):
                    if c == 2:
                        pe.wait_ge(root_read, 3 * h + 1)
                    pe.matmul(core.ps[:, 6 + c % 2, 0:CH], core.ones[:, :], sq[:, c * CH:(c + 1) * CH],
                              start=True, stop=True).then_inc(v_sum_mm, 1)
                if not last:
                    job(2 * h + 2, 0)
                pe.wait_ge(vn_ready, h + 1)
                pe.wait_ge(evac, 2 * h + 4)
                for t in range(9):
                    m = P if t < 8 else T - SEQ
                    mm = pe.transpose(core.ps[0:m, 3 + t // 4, (t % 4) * P:(t % 4 + 1) * P],
                                      vb[:, t * P:t * P + m], core.ident[:, :])
                    if t in (3, 7, 8):
                        mm.then_inc(v_tr, 1)
                pe.wait_ge(masked, 2)
                pe.wait_ge(tok_copied, 3 * h + 3)
                pe.matmul(core.ps[:, 3, 0:NS], vtok[0:NS, 8, :],
                          wb[:, bass.ds(h, 1), :].rearrange("p o t -> p (o t)"), start=True, stop=True
                          ).then_inc(mix_mm, 1)
                for t in range(8):
                    mm = pe.matmul(core.ps[:, 6 + t // 4, (t % 4) * P:(t % 4 + 1) * P], vtok[:, t, :],
                                   wt[:, bass.ds(h, 1), :].rearrange("p o t -> p (o t)"), start=True, stop=True)
                    if t % 4 == 3:
                        mm.then_inc(mix_mm, 1)

            with pe.Fori(0, 7) as h:
                turn(h, False)
            turn(7, True)

        @block.scalar
        def _(act):
            norm.split_act(act)
            norm.squares_act(act)
            act.wait_ge(prep_tr, 1)
            for b in range(2):
                act.copy(wt[:, 4 * b:4 * b + 4, :], core.ps[:, 3 + b, :].rearrange("p (h t) -> p h t", h=4)
                         ).then_inc(prep_copied, 1)
            act.copy(wb[:, :, :], core.ps[0:NS, 5, :].rearrange("p (h t) -> p h t", h=8)).then_inc(prep_copied, 1)
            norm.roots_act(act)
            with act.Fori(0, 8) as h:
                act.wait_ge(evac, 2 * h + 3)
                act.activation(vb[:, :], vb[:, :], ACT.Gelu_apprx_tanh).then_inc(v_gelu, 1)
                act.wait_ge(v_gelu, h + 1)
                act.activation(sq[:, :], vb[:, :], ACT.Square).then_inc(sq_ready, 1)
                w.split_hi(act, n0 + 2 * h + 2, n0 // 2 + h + 1, 0)
                act.preload_act_table_set("natural_log_exp_and_others")
                for c in range(3):
                    act.wait_ge(v_sum_mm, 3 * h + c + 1)
                    act.activation(rv[:, c * CH:(c + 1) * CH], core.ps[:, 6 + c % 2, 0:CH], ACT.Ln,
                                   scale=1.0 / P, bias=EPS).then_inc(root_read, 1)
                act.wait_ge(root_read, 3 * h + 3)
                act.activation(rv[:, :], rv[:, :], ACT.Exp, scale=-0.5).then_inc(root_ready, 1)
                act.wait_ge(evac, 2 * h + 4)
                act.activation(ub[:, :], ub[:, :], ACT.Gelu_apprx_tanh).then_inc(u_gelu, 1)
                w.split_hi(act, n0 + 2 * h + 3, n0 // 2 + h + 1, 1)
                act.wait_ge(tok_free, h + 1)
                act.wait_ge(mix_read, 3 * h + 3)
                for b in range(3):
                    m, n = (P, 4) if b < 2 else (NS, 1)
                    act.wait_ge(v_tr, 3 * h + b + 1)
                    act.activation(vtok[0:m, 4 * b:4 * b + n, :],
                                   core.ps[0:m, 3 + b, 0:n * P].rearrange("p (t c) -> p t c", c=P),
                                   ACT.Copy).then_inc(tok_copied, 1)
                act.wait_ge(tok_copied, 3 * h + 3)
                act.sem_inc(tok_ready, 1)

        @block.vector
        def _(dve):
            o = Order(dve, dve_step)
            dve.sem_inc(evac, 2)
            dve.sem_inc(mix_read, 3)
            norm.split_dve(dve)
            norm.sums_dve(dve)
            norm.scale_dve(dve)
            with dve.Fori(0, 8) as h:
                o.enter(h, 3)
                w.wait_job(dve, n0 + 2 * h)
                dve.wait_ge(mix_read, 3 * h + 3)
                dve.tensor_tensor(chunks(vb[:, :]), core.bank_a[:, :, 0:CH], chunks(core.rb[:, :]), ALU.mult
                                  ).then_inc(evac, 1)
                w.wait_job(dve, n0 + 2 * h + 1)
                dve.tensor_tensor(chunks(ub[:, :]), core.bank_b[:, :, 0:CH], chunks(core.rb[:, :]), ALU.mult
                                  ).then_inc(evac, 1)
                dve.wait_ge(root_ready, h + 1)
                dve.scalar_tensor_tensor(vb[:, :], vb[:, :], core.par[:, bass.ds(h + 64, 1)], rv[:, :],
                                         ALU.mult, ALU.mult).then_inc(vn_ready, 1)
                dve.wait_ge(u_gelu, h + 1)
                tile = uv[:, bass.ds(h, 1), :]
                for use, b in enumerate((2, 0, 1)):
                    if b < 2:
                        dst = tile[:, :, b * 512:(b + 1) * 512].rearrange("p o (n t) -> p (o n) t", t=P)
                        u = ub[:, b * 512:(b + 1) * 512].rearrange("p (n t) -> p n t", t=P)
                        src = core.ps[:, 6 + b, :].rearrange("p (n t) -> p n t", t=P)
                        bias = bs[:, bass.ds(h, 1), :].to_broadcast((P, 4, P))
                    else:
                        dst = tile[:, :, SEQ:SEQ + NS].rearrange("p o (n t) -> p (o n) t", t=SLEN)
                        u = ub[:, SEQ:SEQ + NS].rearrange("p (n t) -> p n t", t=SLEN)
                        src = core.ps[:, 3, 0:NS].rearrange("p (n t) -> p n t", t=SLEN)
                        bias = bs[:, bass.ds(h, 1), 0:SLEN].to_broadcast((P, NSEQ, SLEN))
                    dve.wait_ge(mix_mm, 3 * h + use + 1)
                    o.did(dve.tensor_tensor(dst, src, bias, ALU.add))
                    o.after()
                    dve.tensor_tensor(dst, dst, u, ALU.mult).then_inc(mix_read, 1)
                o.leave(8)
            dve.wait_ge(mix_read, 27)
            o.did(dve.memset(uv[:, :, SEQ + NS:T], 0.0))
    core.slabs += 16


def phase_store(core):
    core.phase = ""
    nc, dr = core.nc, core.dram
    with ExitStack() as ctx:
        ys = ctx.enter_context(nc.sbuf_tensor("y_rows", [P, 9, D], F32))

        def sem(name):
            return core.sem(name + "_store")

        tr_done, act_copied, dve_copied, stored = sem("tr_done"), sem("act_copied"), sem("dve_copied"), sem("stored")
        block = ctx.enter_context(nc.Block())

        @block.sync
        def _(sp):
            yp = dr["y_prompt"][0].rearrange("(t p) n -> t p n", p=P)
            for t in range(9):
                sp.wait_ge(act_copied, t + 1)
                sp.wait_ge(dve_copied, t + 1)
                if t < 8:
                    sp.dma_start(yp[t], ys[:, t, :]).then_inc(stored, 16)
                else:
                    sp.dma_start(dr["y_sample"].rearrange("s t n -> (s t) n"), ys[0:NS, 8, :]).then_inc(stored, 16)
            sp.wait_ge(stored, 144)

        @block.tensor
        def _(pe):
            for n in range(18):
                t, g = n // 2, n % 2
                m = P if t < 8 else T - SEQ
                if n >= 8:
                    pe.wait_ge(dve_copied if g else act_copied, (n - 8) // 2 + 1)
                for q in range(4):
                    mm = pe.transpose(core.ps[0:m, n % 8, q * P:(q + 1) * P],
                                      core.x[:, 4 * g + q, t * P:t * P + m], core.ident[:, :])
                mm.then_inc(tr_done, 1)

        def copy_rows(eng, copy, n, done):
            m = P if n < 16 else NS
            eng.wait_ge(tr_done, n + 1)
            copy(ys[0:m, n // 2, 512 * (n % 2):512 * (n % 2) + 512], core.ps[0:m, n % 8, :]).then_inc(done, 1)

        @block.scalar
        def _(act):
            for n in range(0, 18, 2):
                copy_rows(act, act.copy, n, act_copied)

        @block.vector
        def _(dve):
            for n in range(1, 18, 2):
                copy_rows(dve, dve.tensor_copy, n, dve_copied)


def build(nc, dram):
    with ExitStack() as ctx:
        core = Core(nc, ctx, dram)
        phase_load(core)

        def split_buffers(stack, tag):
            return (stack.enter_context(nc.sbuf_tensor("in_hi" + tag, [P, KT, T], F32R)),
                    stack.enter_context(nc.sbuf_tensor("in_lo" + tag, [P, KT, T], F32R)))

        w_odd, w_odd_out = dram["w_in_odd"][0], dram["w_out_odd"][0]
        with ExitStack() as even:
            mix = even.enter_context(nc.sbuf_tensor("mixed_even", [P, KT, T], F32))
            k_sample = even.enter_context(nc.sbuf_tensor("k_sample_columns", [P, 4, NS], F32))
            with ExitStack() as proj:
                hi, lo = split_buffers(proj, "_even")
                phase_lru(core, hi, lo, mix)
                phase_attention(core, hi, lo, mix, k_sample)
            phase_sample_attention(core, mix, k_sample)
            core.free_sems()
            with ExitStack() as proj:
                hi, lo = split_buffers(proj, "_even_out")
                phase_out(core, hi, lo, mix, dram["w_out_even"][0], "_out_even",
                          (square_slab(dram["w_gate"][0], 0), square_slab(dram["w_up"][0], 0)))
        with ExitStack() as rest:
            hi, lo = split_buffers(rest, "_rest")
            phase_ffn(core, 0, hi, lo, (square_slab(w_odd, D), square_slab(w_odd, 0)))
            with ExitStack() as odd:
                uv = odd.enter_context(nc.sbuf_tensor("mixed_odd", [P, KT, T], F32))
                phase_odd(core, hi, lo, uv, (square_slab(w_odd_out, 0), square_slab(w_odd_out, P)))
                phase_out(core, hi, lo, uv, w_odd_out, "_out_odd",
                          (square_slab(dram["w_gate"][1], 0), square_slab(dram["w_up"][1], 0)))
            phase_ffn(core, 1, hi, lo, ())
        phase_store(core)


OUTS = [("y_prompt", (1, SEQ, D)), ("y_sample", (NSEQ, SLEN, D)),
        ("k_prompt", (1, 1, SEQ, 8, HD)), ("v_prompt", (1, 1, SEQ, 8, HD)),
        ("k_sample", (1, NSEQ, SLEN, 8, HD)), ("v_sample", (1, NSEQ, SLEN, 8, HD)),
        ("lru_h_prompt", (1, 1, 512)), ("lru_h_sample", (1, NSEQ, 512)),
        ("lru_conv_prompt", (1, 1, 3, 512)), ("lru_conv_sample", (1, NSEQ, 3, 512)),
        ("chunk_v_prompt", (1, 1, P, D)), ("chunk_v_sample", (1, NSEQ, SLEN, D)),
        ("ffn_conv_prompt", (2, 1, 2, FF)), ("ffn_conv_sample", (2, NSEQ, 2, FF))]


_INS = ["x_prompt", "x_sample", "cache_k", "cache_v", "state_lru_h", "state_lru_conv", "state_ffn_conv", "page_table",
        "g_mix", "g_ffn", "w_in_even", "g_q", "g_k", "sb_bias", "w_conv_lru", "b_conv_lru", "w_rgate", "b_rgate",
        "w_igate", "b_igate", "lru_lambda", "w_out_even", "w_in_odd", "g_v", "w_spatial", "b_spatial", "w_out_odd",
        "w_gate", "w_up", "w_ffn_conv", "b_ffn_conv", "w_down"]


def kernel(**inputs):
    import numpy as _np
    import concourse.bacc as _bacc
    from concourse import mybir as _mybir
    from concourse.bass_utils import run_bass_kernel_spmd as _run

    nc = _bacc.Bacc("TRN2", target_bir_lowering=False, num_devices=1)
    arrays, dram = {}, {}
    for name in _INS:
        a = _np.ascontiguousarray(inputs[name])
        if a.dtype.kind in "iu":
            a = a.astype(_np.int64)
        arrays[f"in_{name}_dram"] = a
        dram[name] = nc.dram_tensor(f"in_{name}_dram", a.shape, _mybir.dt.from_np(a.dtype), kind="ExternalInput").ap()
    for i, (name, shape) in enumerate(OUTS):
        dram[name] = nc.dram_tensor(f"out_{i}_dram", shape, _mybir.dt.float32, kind="ExternalOutput").ap()
    build(nc, dram)
    r = _run(nc, [arrays], core_ids=[0])
    return tuple(r.results[0][f"out_{i}_dram"] for i in range(len(OUTS)))
```
